# Optimizing a Trainium2 kernel written in Bass

```python
import jax, jax.numpy as jnp
from jax import lax
import numpy as np

'''One inference step of a hybrid decoder trunk (DEPTH layers) for two request groups sharing weights.

Layer (sandwich norm, parallel head groups):
  h = RMSNorm_pre(x); [qA,kA,vA,qB,kB,vB] = h @ w_in  (one combined projection, columns partitioned)
  mixer A: sliding-window GQA (distance 0..128) with learned per-head sinks, partial rotary
  mixer B: dilated sliding-window MHA, branches (128,1),(512,4),(2048,16): keys at distances 0,d,2d,..,window,
           merged per position weighted by branch softmax denominators, partial rotary
  x += RMSNorm_post(concat(RMSNorm(oA), RMSNorm(oB)) @ w_out)
  x += RMSNorm_post(ConvFFN(RMSNorm_pre(x)))   ConvFFN = (gelu(causal_dwconv3(h@w_gate)) * (h@w_up)) @ w_down

Inputs: x_prompt (BATCH, SEQ, D_MODEL), positions 0..SEQ-1; x_sample (DEC_BATCH, DEC_SEQ, D_MODEL), positions PAST_LEN..;
  cache_a_k, cache_a_v (DEPTH, DEC_BATCH, min(WINDOW_A, PAST_LEN), N_KV_A, HEAD_DIM)   last rows of mixer-A keys (rotated) / values
  cache_b_k, cache_b_v (DEPTH, DEC_BATCH, min(WINDOW_B_MAX, PAST_LEN), N_HEADS_B, HEAD_DIM)
  state_conv (DEPTH, DEC_BATCH, CONV_W-1, D_FF)   last up-projected (gate branch) rows of the ConvFFN
Returns (y_prompt (BATCH,SEQ,D_MODEL), y_sample (DEC_BATCH,DEC_SEQ,D_MODEL),
  a_k_prompt, a_v_prompt (DEPTH,BATCH,min(WINDOW_A,SEQ),N_KV_A,HEAD_DIM),
  b_k_prompt, b_v_prompt (DEPTH,BATCH,min(WINDOW_B_MAX,SEQ),N_HEADS_B,HEAD_DIM),
  conv_prompt (DEPTH,BATCH,CONV_W-1,D_FF),
  a_k_sample, a_v_sample (DEPTH,DEC_BATCH,DEC_SEQ,N_KV_A,HEAD_DIM),
  b_k_sample, b_v_sample (DEPTH,DEC_BATCH,DEC_SEQ,N_HEADS_B,HEAD_DIM),
  conv_sample (DEPTH,DEC_BATCH,CONV_W-1,D_FF)).
'''

D_MODEL = 2048
BATCH = 1
SEQ = 256
DEPTH = 1
DEC_BATCH = 8
DEC_SEQ = 1
PAST_LEN = 2048
PAGE_SIZE = 128

HEAD_DIM = 64
N_HEADS_A = 16
N_KV_A = 2
G_A = N_HEADS_A // N_KV_A
N_HEADS_B = 16
D_A = N_HEADS_A * HEAD_DIM
D_B = N_HEADS_B * HEAD_DIM
D_MIX = D_A + D_B
D_IN = D_A + 2 * N_KV_A * HEAD_DIM + 3 * D_B
WINDOW_A = 128
DILATIONS = ((128, 1), (512, 4), (2048, 16))
WINDOW_B_MAX = 2048
ROT_DIM = HEAD_DIM // 4
ROPE_THETA = 500000.0
D_FF = 5632
CONV_W = 3
BLOCK = 128
EPS = 1e-6
NEG = -1e30

kernel_name = 'hymba_swa_sink_dilated_convffn_step'

def _rms_norm(x, g):
    xf = x.astype(jnp.float32)
    y = xf * lax.rsqrt(jnp.mean(xf * xf, axis=-1, keepdims=True) + EPS)
    return (y * g.astype(jnp.float32)).astype(x.dtype)

def _rope(x, pos):
    half = ROT_DIM // 2
    inv = ROPE_THETA ** (-jnp.arange(half, dtype=jnp.float32) * (2.0 / ROT_DIM))
    ang = pos.astype(jnp.float32)[:, None] * inv[None, :]
    shape = (ang.shape[0],) + (1,) * (x.ndim - 3) + (half,)
    c = jnp.cos(ang).reshape(shape)
    s = jnp.sin(ang).reshape(shape)
    xr = x[..., :ROT_DIM].astype(jnp.float32)
    x1, x2 = xr[..., :half], xr[..., half:]
    rot = jnp.concatenate([x1 * c - x2 * s, x2 * c + x1 * s], axis=-1).astype(x.dtype)
    return jnp.concatenate([rot, x[..., ROT_DIM:]], axis=-1)

def _project(h, w_in, pos):
    N, L, _ = h.shape
    z = h @ w_in
    cuts = list(np.cumsum([D_A, N_KV_A * HEAD_DIM, N_KV_A * HEAD_DIM, D_B, D_B]))
    qa, ka, va, qb, kb, vb = jnp.split(z, cuts, axis=-1)
    qa = _rope(qa.reshape(N, L, N_KV_A, G_A, HEAD_DIM), pos)
    ka = _rope(ka.reshape(N, L, N_KV_A, HEAD_DIM), pos)
    va = va.reshape(N, L, N_KV_A, HEAD_DIM)
    qb = _rope(qb.reshape(N, L, N_HEADS_B, HEAD_DIM), pos)
    kb = _rope(kb.reshape(N, L, N_HEADS_B, HEAD_DIM), pos)
    vb = vb.reshape(N, L, N_HEADS_B, HEAD_DIM)
    return qa, ka, va, qb, kb, vb

def _banded(q, k, v, max_dist):
    N, L, Hk, G, Dh = q.shape
    nb = -(-L // BLOCK)
    Lp = nb * BLOCK
    pad = Lp - L
    qf = jnp.pad(q.astype(jnp.float32), ((0, 0), (0, pad), (0, 0), (0, 0), (0, 0)))
    kf = jnp.pad(k.astype(jnp.float32), ((0, 0), (0, pad), (0, 0), (0, 0)))
    vf = jnp.pad(v.astype(jnp.float32), ((0, 0), (0, pad), (0, 0), (0, 0)))
    qb = qf.reshape(N, nb, BLOCK, Hk, G, Dh)
    kb = kf.reshape(N, nb, BLOCK, Hk, Dh)
    vb = vf.reshape(N, nb, BLOCK, Hk, Dh)
    kk = jnp.concatenate([jnp.pad(kb, ((0, 0), (1, 0), (0, 0), (0, 0), (0, 0)))[:, :-1], kb], axis=2)
    vv = jnp.concatenate([jnp.pad(vb, ((0, 0), (1, 0), (0, 0), (0, 0), (0, 0)))[:, :-1], vb], axis=2)
    s = jnp.einsum('nbqhgd,nbkhd->nbhgqk', qb, kk) * (HEAD_DIM ** -0.5)
    blk = jnp.arange(nb)[:, None, None]
    qi = jnp.arange(BLOCK)[None, :, None]
    kj = jnp.arange(2 * BLOCK)[None, None, :]
    dist = BLOCK + qi - kj
    kpos = (blk - 1) * BLOCK + kj
    valid = (dist >= 0) & (dist <= max_dist) & (kpos >= 0)
    s = jnp.where(valid[None, :, None, None], s, NEG)
    m = jnp.max(s, axis=-1)
    p = jnp.exp(s - m[..., None])
    l = jnp.sum(p, axis=-1)
    num = jnp.einsum('nbhgqk,nbkhd->nbqhgd', p, vv).reshape(N, Lp, Hk, G, Dh)[:, :L]
    m = m.transpose(0, 1, 4, 2, 3).reshape(N, Lp, Hk, G)[:, :L]
    l = l.transpose(0, 1, 4, 2, 3).reshape(N, Lp, Hk, G)[:, :L]
    return num, m, l

def _local_sample(q, k_all, v_all, qpos, kpos, max_dist):
    s = jnp.einsum('nqhgd,nkhd->nhgqk', q.astype(jnp.float32), k_all.astype(jnp.float32)) * (HEAD_DIM ** -0.5)
    dist = qpos[:, None] - kpos[None, :]
    valid = (dist >= 0) & (dist <= max_dist)
    s = jnp.where(valid, s, NEG)
    m = jnp.max(s, axis=-1)
    p = jnp.exp(s - m[..., None])
    l = jnp.sum(p, axis=-1)
    num = jnp.einsum('nhgqk,nkhd->nqhgd', p, v_all.astype(jnp.float32))
    return num, m.transpose(0, 3, 1, 2), l.transpose(0, 3, 1, 2)

def _sink_normalise(num, m, l, sink):
    sink = sink.astype(jnp.float32)
    m2 = jnp.maximum(m, sink)
    a = jnp.exp(m - m2)
    den = l * a + jnp.exp(sink - m2)
    return num * (a / den)[..., None]

def _dilated_prompt(q, k, v, window, dil):
    N, L, H, Dh = q.shape
    Ld = L // dil

    def fold(t):
        return t.reshape(N, Ld, dil, H, Dh).transpose(0, 2, 1, 3, 4).reshape(N * dil, Ld, H, Dh)

    num, m, l = _banded(fold(q)[:, :, :, None], fold(k), fold(v), window // dil)
    num = num[:, :, :, 0].reshape(N, dil, Ld, H, Dh).transpose(0, 2, 1, 3, 4).reshape(N, L, H, Dh)
    m = m[..., 0].reshape(N, dil, Ld, H).transpose(0, 2, 1, 3).reshape(N, L, H)
    l = l[..., 0].reshape(N, dil, Ld, H).transpose(0, 2, 1, 3).reshape(N, L, H)
    return num, m, l

def _dilated_sample(q, k_all, v_all, n_buf, window, dil):
    S = q.shape[1]
    nj = window // dil + 1
    idx = n_buf + jnp.arange(S)[:, None] - dil * jnp.arange(nj)[None, :]
    valid = idx >= 0
    idx = jnp.maximum(idx, 0)
    kg = k_all[:, idx].astype(jnp.float32)
    vg = v_all[:, idx].astype(jnp.float32)
    s = jnp.einsum('nqhd,nqjhd->nqhj', q.astype(jnp.float32), kg) * (HEAD_DIM ** -0.5)
    s = jnp.where(valid[None, :, None, :], s, NEG)
    m = jnp.max(s, axis=-1)
    p = jnp.exp(s - m[..., None])
    l = jnp.sum(p, axis=-1)
    num = jnp.einsum('nqhj,nqjhd->nqhd', p, vg)
    return num, m, l

def _merge_dilations(parts):
    m_star = jnp.max(jnp.stack([p[1] for p in parts]), axis=0)
    num = sum(jnp.exp(p[1] - m_star)[..., None] * p[0] for p in parts)
    den = sum(jnp.exp(p[1] - m_star) * p[2] for p in parts)
    return num / den[..., None]

def _mixer_and_ffn(x, o_a, o_b, prev_conv, w_out, g_out_a, g_out_b, g_post_mix, g_pre_ffn, g_post_ffn,
                   w_gate, w_up, conv_w, conv_b, w_down):
    N, L, _ = x.shape
    dt = x.dtype
    o = jnp.concatenate([_rms_norm(o_a.reshape(N, L, D_A).astype(dt), g_out_a),
                         _rms_norm(o_b.reshape(N, L, D_B).astype(dt), g_out_b)], axis=-1)
    x = x + _rms_norm(o @ w_out, g_post_mix).astype(dt)
    h = _rms_norm(x, g_pre_ffn)
    u = h @ w_gate
    up = h @ w_up
    u_pad = jnp.concatenate([prev_conv.astype(u.dtype), u], axis=1)
    c = conv_b + sum(conv_w[j] * u_pad[:, j:j + L] for j in range(CONV_W))
    y = (jax.nn.gelu(c, approximate=True) * up) @ w_down
    x = x + _rms_norm(y, g_post_ffn).astype(dt)
    return x, u_pad[:, L:]

def _layer_prompt(x, w_in, w_out, attn_sinks, g_out_a, g_out_b, g_pre_mix, g_post_mix, g_pre_ffn, g_post_ffn,
                  w_gate, w_up, conv_w, conv_b, w_down):
    N, L, _ = x.shape
    pos = jnp.arange(L, dtype=jnp.int32)
    h = _rms_norm(x, g_pre_mix)
    qa, ka, va, qb, kb, vb = _project(h, w_in, pos)
    num, m, l = _banded(qa, ka, va, WINDOW_A)
    o_a = _sink_normalise(num, m, l, attn_sinks)
    o_b = _merge_dilations([_dilated_prompt(qb, kb, vb, w, d) for w, d in DILATIONS])
    prev = jnp.zeros((N, CONV_W - 1, D_FF), x.dtype)
    x, conv_state = _mixer_and_ffn(x, o_a, o_b, prev, w_out, g_out_a, g_out_b, g_post_mix, g_pre_ffn,
                                   g_post_ffn, w_gate, w_up, conv_w, conv_b, w_down)
    na = min(WINDOW_A, L)
    nbf = min(WINDOW_B_MAX, L)
    return x, (ka[:, L - na:], va[:, L - na:], kb[:, L - nbf:], vb[:, L - nbf:], conv_state)

def _layer_sample(x, c_a_k, c_a_v, c_b_k, c_b_v, c_conv, w_in, w_out, attn_sinks, g_out_a, g_out_b,
                  g_pre_mix, g_post_mix, g_pre_ffn, g_post_ffn, w_gate, w_up, conv_w, conv_b, w_down):
    N, S, _ = x.shape
    pos = PAST_LEN + jnp.arange(S, dtype=jnp.int32)
    h = _rms_norm(x, g_pre_mix)
    qa, ka, va, qb, kb, vb = _project(h, w_in, pos)
    na = c_a_k.shape[1]
    ka_all = jnp.concatenate([c_a_k.astype(ka.dtype), ka], axis=1)
    va_all = jnp.concatenate([c_a_v.astype(va.dtype), va], axis=1)
    kpos = PAST_LEN - na + jnp.arange(na + S, dtype=jnp.int32)
    num, m, l = _local_sample(qa, ka_all, va_all, pos, kpos, WINDOW_A)
    o_a = _sink_normalise(num, m, l, attn_sinks)
    nbf = c_b_k.shape[1]
    kb_all = jnp.concatenate([c_b_k.astype(kb.dtype), kb], axis=1)
    vb_all = jnp.concatenate([c_b_v.astype(vb.dtype), vb], axis=1)
    o_b = _merge_dilations([_dilated_sample(qb, kb_all, vb_all, nbf, w, d) for w, d in DILATIONS])
    x, conv_state = _mixer_and_ffn(x, o_a, o_b, c_conv, w_out, g_out_a, g_out_b, g_post_mix, g_pre_ffn,
                                   g_post_ffn, w_gate, w_up, conv_w, conv_b, w_down)
    return x, (ka, va, kb, vb, conv_state)

def setup_inputs(seed: int = 0) -> dict:
    key = jax.random.key(seed)
    ks = jax.random.split(key, 24)

    def nrm(k, shape, scale):
        return jax.random.normal(k, shape, jnp.float32) * scale

    na = min(WINDOW_A, PAST_LEN)
    nbf = min(WINDOW_B_MAX, PAST_LEN)
    return {
        'x_prompt': nrm(ks[0], (BATCH, SEQ, D_MODEL), 1.0),
        'x_sample': nrm(ks[1], (DEC_BATCH, DEC_SEQ, D_MODEL), 1.0),
        'cache_a_k': nrm(ks[2], (DEPTH, DEC_BATCH, na, N_KV_A, HEAD_DIM), 1.0),
        'cache_a_v': nrm(ks[3], (DEPTH, DEC_BATCH, na, N_KV_A, HEAD_DIM), 1.0),
        'cache_b_k': nrm(ks[4], (DEPTH, DEC_BATCH, nbf, N_HEADS_B, HEAD_DIM), 1.0),
        'cache_b_v': nrm(ks[5], (DEPTH, DEC_BATCH, nbf, N_HEADS_B, HEAD_DIM), 1.0),
        'state_conv': nrm(ks[6], (DEPTH, DEC_BATCH, CONV_W - 1, D_FF), 1.0),
        'w_in': nrm(ks[7], (DEPTH, D_MODEL, D_IN), D_MODEL ** -0.5),
        'w_out': nrm(ks[8], (DEPTH, D_MIX, D_MODEL), D_MIX ** -0.5),
        'attn_sinks': nrm(ks[9], (DEPTH, N_KV_A, G_A), 0.5),
        'g_out_a': 1.0 + nrm(ks[10], (DEPTH, D_A), 0.05),
        'g_out_b': 1.0 + nrm(ks[11], (DEPTH, D_B), 0.05),
        'g_pre_mix': 1.0 + nrm(ks[12], (DEPTH, D_MODEL), 0.05),
        'g_post_mix': 1.0 + nrm(ks[13], (DEPTH, D_MODEL), 0.05),
        'g_pre_ffn': 1.0 + nrm(ks[14], (DEPTH, D_MODEL), 0.05),
        'g_post_ffn': 1.0 + nrm(ks[15], (DEPTH, D_MODEL), 0.05),
        'w_gate': nrm(ks[16], (DEPTH, D_MODEL, D_FF), D_MODEL ** -0.5),
        'w_up': nrm(ks[17], (DEPTH, D_MODEL, D_FF), D_MODEL ** -0.5),
        'conv_w': nrm(ks[18], (DEPTH, CONV_W, D_FF), CONV_W ** -0.5),
        'conv_b': nrm(ks[19], (DEPTH, D_FF), 0.02),
        'w_down': nrm(ks[20], (DEPTH, D_FF, D_MODEL), D_FF ** -0.5),
    }

def reference(x_prompt, x_sample, cache_a_k, cache_a_v, cache_b_k, cache_b_v, state_conv, w_in, w_out,
              attn_sinks, g_out_a, g_out_b, g_pre_mix, g_post_mix, g_pre_ffn, g_post_ffn, w_gate, w_up,
              conv_w, conv_b, w_down):
    xp, xs = x_prompt, x_sample
    outs_p = [[] for _ in range(5)]
    outs_s = [[] for _ in range(5)]
    for i in range(DEPTH):
        lw = (w_in[i], w_out[i], attn_sinks[i], g_out_a[i], g_out_b[i], g_pre_mix[i], g_post_mix[i],
              g_pre_ffn[i], g_post_ffn[i], w_gate[i], w_up[i], conv_w[i], conv_b[i], w_down[i])
        xp, st_p = _layer_prompt(xp, *lw)
        xs, st_s = _layer_sample(xs, cache_a_k[i], cache_a_v[i], cache_b_k[i], cache_b_v[i], state_conv[i], *lw)
        for j in range(5):
            outs_p[j].append(st_p[j])
            outs_s[j].append(st_s[j])
    sp = [jnp.stack(o, axis=0) for o in outs_p]
    ss = [jnp.stack(o, axis=0) for o in outs_s]
    return (xp, xs, sp[0], sp[1], sp[2], sp[3], sp[4], ss[0], ss[1], ss[2], ss[3], ss[4])


_drawn_inputs = setup_inputs


def setup_inputs(seed=0):
    import zlib

    import numpy as np

    out = dict(_drawn_inputs(seed))
    spreads = {}
    factors = {'attn_sinks': 4.401, 'conv_b': 4.979}
    for name, (base, spread) in spreads.items():
        noise = np.random.default_rng([zlib.crc32(name.encode()), seed]).standard_normal(out[name].shape)
        drawn = base * np.exp(spread * noise) if base else spread * noise
        out[name] = __import__('jax').numpy.asarray(drawn.astype(out[name].dtype))
    for name, factor in factors.items():
        out[name] = (out[name] * factor).astype(out[name].dtype)
    return out
```

```python
from contextlib import ExitStack

import numpy as np

import concourse.bass as bass
from concourse import mybir

F32 = mybir.dt.float32
F32R = mybir.dt.float32r
ALU = mybir.AluOpType
ACT = mybir.ActivationFunctionType
AX = mybir.AxisListType

P = 128
D_MODEL, D_FF = 2048, 5632
HD, H_A, KV_A, H_B = 64, 16, 2, 16
SEQ, NDEC, PAST = 256, 8, 2048
TOK = SEQ + NDEC
ROT, THETA, EPS = 16, 500000.0, 1e-6
SCALE = HD ** -0.5
WINDOW_A = 128
DILATIONS = ((128, 1), (512, 4), (2048, 16))
NEG = 1e30

MT = D_MODEL // P
OT = 8
FT = D_FF // P
CH = 1024
RING = 4
G_IN = 17
G_OUT = D_MODEL // 256
G_FF = D_FF // 256
N_IN, N_OUTA, N_OUTB, N_GU, N_DOWN = G_IN * 4, G_OUT * 2, G_OUT * 2, G_FF * 8, 2 * FT
CHUNKS = N_IN + N_OUTA + N_OUTB + N_GU + N_DOWN
SUMS = MT // 2 + 1
STEPS = N_IN + N_OUTA
N_ATT = STEPS
B_OUTB = STEPS
B_GU = B_OUTB + N_OUTB
B_DOWN = B_GU + N_GU

KEYS_B = 320
KB = KEYS_B + 1
KA = WINDOW_A + 1
KSPLIT_B = ((0, 128), (128, 256), (256, KB))
KSPLIT_A = ((0, 65), (65, KA))

C_GPM, C_GQM, C_GPF, C_GQF = 0, 16, 32, 48
C_GOUT = 64
C_CW = 80
C_CB = C_CW + 3 * FT
C_ST = C_CB + FT
C_SINK = C_ST + FT * 16
C_SROW = C_SINK + H_A
N_PAR = C_SROW + 1
T_MA, T_MB, T_COS, T_SIN, T_MD = 0, 384, 768, 768 + TOK, 768 + 2 * TOK
N_TAB = T_MD + KB

SWAP = list(range(8, 16)) + list(range(0, 8)) + list(range(16, 32))


def groups_in():
    order = [("kvA", 0, 4)] + [("qA", t, t) for t in range(4)]
    for t in range(4):
        order += [("qB", t, 5 + t), ("kB", t, 9 + t), ("vB", t, 13 + t)]
    return order


GROUPS = groups_in()
GI = {(kind, t): gi for gi, (kind, t, _) in enumerate(GROUPS)}


def q_group(T):
    return GI[("qA", T)] if T < 4 else GI[("qB", T - 4)]


def group_end(gi):
    return 4 * (gi + 1) if gi < G_IN else N_IN + 2 * (gi - G_IN + 1)


def make_plan():
    plan = {n: [] for n in range(-1, N_ATT + 1)}
    add = lambda n, *s: plan[n].append(s)
    for gi in range(G_IN):
        add(4 * gi + 4, "evac", gi)
    for g in range(G_OUT):
        add(N_IN + 2 * g + 2, "evac", G_IN + g)
    add(2, "ss")
    add(5, "vtr", -1)
    add(6, "vdec", -1)
    for t in range(4):
        n = 4 * (t + 1) + 4
        for a in range(4):
            add(n + 1 + a, "S", t, a)
            add(n + 2 + a, "T", t, a)
            add(n + 3 + a, "V", t, a)
        add(n + 5, "L", t)
        add(n + 6, "O", t)
    add(22, "aS")
    add(23, "aT")
    add(25, "aR")
    add(26, "aV")
    add(27, "N", 0)
    for j in range(OT):
        add(28 + j, "W", 0, j)
    add(36, "ND", 0)
    for t in range(4):
        e = 32 + 12 * t
        T = 4 + t
        add(e + 1, "vtr", T)
        add(e + 1, "vdec", T)
        gap = 3 if t < 3 else 1
        for a in range(4):
            add(e + 2 + gap * a, "S", T, a)
            add(e + 3 + gap * a, "T", T, a)
            add(e + 4 + gap * a, "V", T, a)
        add(e + 4 + 3 * gap, "O", T)
        for v in range(2):
            u = 2 * t + v
            b = e + 2 + (5 if t < 3 else 2) * v
            add(b - 1 if v == 0 else b, "bQ", u)
            add(b, "bS", u)
            add(b + 1, "bT", u)
            add(b + 3 if t < 3 else b + 2, "bR", u)
            add(b + 4 if t < 3 else b + 3, "bV", u)
    add(77, "ND", 1)
    add(76, "N", 1)
    for j in range(OT):
        add(77 + j if 77 + j <= N_ATT else N_ATT, "W", 1, j)
    return plan


PLAN = make_plan()
ORDER = {}
for _n in sorted(PLAN):
    for _s in PLAN[_n]:
        ORDER.setdefault(_s[0], []).append(_s[1:])
MISC = [s for n in sorted(PLAN) for s in PLAN[n]
        if s[0] in ("ss", "vtr", "vdec", "aS", "aT", "aR", "aV", "W", "ND", "bS", "bT", "bR", "bV")]


def number(kind, *args):
    return ORDER[kind].index(args) + 1


def misc(kind, *args):
    return MISC.index((kind,) + args)


class Line:

    def __init__(self, eng, sem):
        self.eng, self.sem, self.n, self.at = eng, sem, 0, 0

    def do(self, ins):
        ins.then_inc(self.sem, 1)
        self.n += 1
        return self.n

    def need(self, n):
        self.eng.wait_ge(self.sem, self.at + n)

    def step(self, ins):
        self.need(self.do(ins))

    def loop(self, i, per):
        self.at, self.start, self.per = i * per, self.n, per

    def end(self, trips):
        assert self.n - self.start == self.per, (self.n - self.start, self.per)
        self.at = 0
        self.n = self.start + trips * self.per



def number_oh(kind, *args):
    return [s for n in sorted(PLAN) for s in PLAN[n] if s[0] in ("W", "ND")].index((kind,) + args) + 1


def build(nc, d):
    ctx = ExitStack()
    with ctx:
        def sem(name):
            return ctx.enter_context(nc.semaphore(name))

        def sb(name, shape, dt=F32, into=ctx):
            return into.enter_context(nc.sbuf_tensor(name, shape, dt))

        xT = sb("xT", [P, MT, TOK])
        raw = sb("raw", [P, RING, CH])
        wh = sb("wh", [P, RING, CH], F32R)
        wl = sb("wl", [P, RING, CH], F32R)
        par = sb("par", [P, N_PAR])
        ident = sb("ident", [P, P])
        ones = sb("ones", [P, P])
        eps = sb("eps", [P, 1])
        rB = sb("rB", [P, TOK])
        rms = sb("rms", [P, TOK])
        hh = sb("hh", [P, MT, TOK], F32R)
        with ExitStack() as over:
            hl = sb("hl", [P, MT, TOK], F32R, over)
        yT = sb("yT", [P, MT, TOK])
        with ExitStack() as att:
            def sa(name, shape, dt=F32):
                return sb(name, shape, dt, att)
            tab = sa("tab", [P, N_TAB])
            oAh = sa("oAh", [P, OT, TOK], F32R)
            oAl = sa("oAl", [P, OT, TOK], F32R)
            qs = sa("qs", [P, 2, 2, TOK])
            ks = sa("ks", [P, 2, 2, TOK])
            vT = sa("vT", [P, 2, TOK])
            vn = sa("vn", [P, 2, 2, 256])
            vdec = sa("vdec", [NDEC, 256])
            kA = sa("kA", [P, TOK])
            kdup = sa("kdup", [P, KV_A, TOK])
            vnA = sa("vnA", [P, 2, P])
            onat = sa("onat", [P, 2, OT * P])
            Sm = sa("Sm", [P, 2, 384])
            Pr = sa("Pr", [P, 2, 384])
            PT = sa("PT", [P, 2, 384])
            r1 = sa("r1", [P, 2, TOK])
            r2 = sa("r2", [P, 2, TOK])
            sh = sa("sh", [P, 2, TOK])
            junk = sh[:, :, 0:256]
            small = sa("small", [P, 128])
            od = sa("od", [P, 4, OT, NDEC])
            rd = sa("rd", [P, 3, NDEC])
            bq = sa("bq", [P, 2, NDEC, 2])
            bSc = sa("bSc", [P, 48])
            bSm = sa("bSm", [16, KB])
            bP = sa("bP", [16, KB])
            bPT = sa("bPT", [P, 48])
            with ExitStack() as a2:
                xsq = sb("xsq", [P, MT, TOK], F32, a2)
            with ExitStack() as a2:
                KtA = sb("KtA", [P, NDEC, KA], F32, a2)
                VtA = sb("VtA", [65, 2, NDEC, P], F32, a2)
                qA = sb("qA", [P, NDEC, H_A], F32, a2)
                aSc = sb("aSc", [65, 256], F32, a2)
                aP = sb("aP", [P, KA], F32, a2)
                aPT = sb("aPT", [65, 256], F32, a2)
            with ExitStack() as a2:
                Kd = sb("Kd", [P, 2, NDEC, KB], F32, a2)
                Vd = sb("Vd", [P, 3, NDEC, P], F32, a2)
        NU = SEQ + 2 + 3 * NDEC
        with ExitStack() as ffn:
            gh = sb("gh", [P, FT, TOK], F32R, ffn)
            gl = sb("gl", [P, FT, TOK], F32R, ffn)
            U = sb("U", [P, 2, NU], F32, ffn)
            cv = sb("cv", [P, 2, NU - 2], F32, ffn)
            ge = sb("ge", [P, 2, TOK], F32, ffn)
            up = sb("up", [P, 2, TOK], F32, ffn)
            co = sb("co", [P, FT, 2 + 2 * NDEC], F32, ffn)
            sq, sqa = ge, up
        U_dec = U[:, :, SEQ + 2:NU].rearrange("p k (s c) -> p k s c", c=3)

        def per_head(c):
            return small[:, c:c + 16].rearrange("p (t b a) -> p t b a", t=2, b=2)
        mn, ll, es, rl = (per_head(c) for c in (0, 16, 32, 48))
        ss4 = small[:, 64:68].rearrange("p (b c) -> p b c", b=2)
        ss2, rm2, ri2 = small[:, 68:70], small[:, 70:72], small[:, 72:74]
        amn, al, aes, ari = (small[:, c:c + 1] for c in (74, 75, 76, 77))
        bmn, bl, bri = (small[0:16, c:c + 1] for c in (78, 79, 80))
        sinkn = small[:, 82:82 + H_A + 1]

        ps = ctx.enter_context(nc.psum_tensor("ps", [P, 8, 512], F32))
        B_S, B_T, B_O, B_M = 4, 5, 6, 7

        x_landed = [sem(f"x_landed{c}") for c in range(4)]
        par_landed = sem("par_landed")
        tab_landed = sem("tab_landed")
        raw_landed = [sem(f"raw_landed{c}") for c in range(RING)]
        hi_ready = sem("hi_ready")
        lo_ready = sem("lo_ready")
        weights_used = sem("weights_used")
        xh_ready = sem("xh_ready")
        xl_ready = sem("xl_ready")
        const_ready = sem("const_ready")
        xsq_ready = sem("xsq_ready")
        evac_done = sem("evac_done")
        misc_ready = sem("misc_ready")
        misc_free = sem("misc_free")
        scores_ready = sem("scores_ready")
        masked_ready = sem("masked_ready")
        exp_ready = sem("exp_ready")
        pt_ready = sem("pt_ready")
        pt_copied = sem("pt_copied")
        pv_ready = sem("pv_ready")
        o_taken = sem("o_taken")
        sinkarg_ready = sem("sinkarg_ready")
        sinkexp_ready = sem("sinkexp_ready")
        kv_stored = [sem(f"kv_stored{c}") for c in range(2)]
        v_stored = sem("v_stored")
        KtA_landed, VtA_landed, VtA_full = sem("KtA_landed"), sem("VtA_landed"), sem("VtA_full")
        Kd_landed = [sem(f"Kd_landed{c}") for c in range(2)]
        Vd_landed, Vd_full = sem("Vd_landed"), sem("Vd_full")
        norm_a = sem("norm_a")
        onat_scaled = sem("onat_scaled")
        oh_ready, ol_ready = sem("oh_ready"), sem("ol_ready")
        od_sq = sem("od_sq")
        od_sum = sem("od_sum")
        od_gained = sem("od_gained")
        aq_ready = sem("aq_ready")
        a_copied, a_min, a_exp, a_p, a_pt = (sem(n) for n in ("a_copied", "a_min", "a_exp", "a_p", "a_pt"))
        bq_ready = sem("bq_ready")
        b_copied, b_min, b_exp, b_p, b_pt = (sem(n) for n in ("b_copied", "b_min", "b_exp", "b_p", "b_pt"))
        vn_ready = sem("vn_ready")
        vdec_ready = sem("vdec_ready")
        ysq_ready, ysq_used = sem("ysq_ready"), sem("ysq_used")
        x1_ready, h2h_ready, h2l_ready = sem("x1_ready"), sem("h2h_ready"), sem("h2l_ready")
        sum_ready = sem("sum_ready")
        rB_ready = sem("rB_ready")
        state_ready, u_ready, tap_ready, conv_ready = (sem(n) for n in ("state_ready", "u_ready", "tap_ready", "conv_ready"))
        u_kept = sem("u_kept")
        gelu_ready, up_taken, g_ready, gh_ready, gl_ready = (
            sem(n) for n in ("gelu_ready", "up_taken", "g_ready", "gh_ready", "gl_ready"))
        down_done = sem("down_done")
        down_v, down_a = sem("down_v"), sem("down_a")
        out_ready, stored, other_stored = sem("out_ready"), sem("stored"), sem("other_stored")
        dve_line, act_line, pool_line = sem("dve_line"), sem("act_line"), sem("pool_line")

        block = ctx.enter_context(nc.Block())

        def chunk(base, i, per, j):
            return i * per + (base + j), (base + j) % RING, i * (per // RING) + (base + j) // RING

        def heads_of(T, a):
            return slice(64 * (a % 2), 64 * (a % 2) + 64), a // 2

        def misc_users(kind, *args):
            return misc(kind, *args)

        @block.sync
        def _(sp):
            def load(c, src):
                n, slot, _ = c
                if not isinstance(n, int) or n >= RING:
                    sp.wait_ge(lo_ready, n - (RING - 1))
                sp.dma_start(raw[:, slot], src).then_inc(raw_landed[slot], 16)

            sp.dma_start(xT[:, 0:4], d["x"][:, 0:4]).then_inc(x_landed[0], 16)
            sp.dma_start(par[:], d["par"]).then_inc(par_landed, 16)
            load(chunk(0, 0, 4, 0), d["w_in"][GROUPS[0][2], 0])
            for c in range(1, 4):
                sp.dma_start(xT[:, 4 * c:4 * c + 4], d["x"][:, 4 * c:4 * c + 4]).then_inc(x_landed[c], 16)
                load(chunk(0, 0, 4, c), d["w_in"][GROUPS[0][2], c])
            sp.dma_start(ident[:], d["ident"]).then_inc(tab_landed, 16)
            sp.dma_start(tab[:], d["tab"]).then_inc(tab_landed, 16)
            for gi in range(1, G_IN):
                for c in range(4):
                    load(chunk(4 * gi, 0, 4, c), d["w_in"][GROUPS[gi][2], c])
            with sp.Fori(0, (N_OUTA + N_OUTB) // 4) as i:
                for j in range(4):
                    load(chunk(N_IN, i, 4, j), d["w_out"][i * 4 + j])
            with sp.Fori(0, G_FF) as i:
                for j in range(4):
                    load(chunk(B_GU, i, 8, j), d["w_gate"][i * 4 + j])
                for j in range(4):
                    load(chunk(B_GU, i, 8, 4 + j), d["w_up"][i * 4 + j])
            with sp.Fori(0, N_DOWN // 4) as i:
                for j in range(4):
                    load(chunk(B_DOWN, i, 4, j), d["w_down"][i * 4 + j])
            for c in range(4):
                sp.wait_ge(out_ready, c + 1)
                sp.dma_start(d["out_y"][:, 4 * c:4 * c + 4], yT[:, 4 * c:4 * c + 4]).then_inc(stored, 16)
            sp.wait_ge(stored, 64)

        @block.scalar
        def _(act):
            line = Line(act, act_line)

            def split(c):
                n, slot, lap = c
                act.wait_ge(raw_landed[slot], lap * 16 + 16)
                if not isinstance(n, int) or n >= RING:
                    act.wait_ge(weights_used, n - (RING - 1))
                nc.scalar.copy(wh[:, slot], raw[:, slot]).then_inc(hi_ready, 1)

            def free_misc(ins):
                ins.then_inc(misc_free, 1)

            def stage(kind, *a):
                if kind == "ss":
                    act.wait_ge(misc_ready, misc(kind, *a) + 1)
                    act.wait_ge(const_ready, 1)
                    free_misc(nc.scalar.activation(rms[:], ps[:, B_M, 0:TOK], ACT.Sqrt, bias=eps[:], scale=1.0 / D_MODEL))
                elif kind == "vtr":
                    T, = a
                    act.wait_ge(misc_ready, misc(kind, *a) + 1)
                    if T >= 6:
                        act.wait_ge(pv_ready, number("V", T - 2, 3))
                    if T < 0:
                        nc.scalar.copy(vnA[:], ps[:, B_M, 0:256].rearrange("p (b c) -> p b c", b=2)).then_inc(misc_free, 1)
                    else:
                        nc.scalar.copy(vn[:, T % 2], ps[:, B_M].rearrange("p (b c) -> p b c", b=2)).then_inc(misc_free, 1)
                elif kind == "vdec":
                    T, = a
                    act.wait_ge(misc_ready, misc(kind, *a) + 1)
                    if T == 4:
                        act.wait_ge(VtA_full, 16)
                    elif T > 4:
                        act.wait_ge(Vd_full, 16 * 2 * (T - 4))
                    w = P if T < 0 else 256
                    nc.scalar.copy(vdec[:, 0:w], ps[0:NDEC, B_M, 0:w]).then_inc(misc_free, 1)
                elif kind == "S":
                    T, h = a
                    n = number(kind, *a)
                    p = n % 2
                    act.wait_ge(masked_ready, n)
                    if n > 2:
                        act.wait_ge(pt_ready, n - 2)
                    line.do(nc.scalar.activation(Pr[:, p, 0:P], Sm[:, p, 0:P], ACT.Exp, scale=-1.0,
                                                 bias=mn[:, T % 2, 0, h:h + 1], accum_out=ll[:, T % 2, 0, h:h + 1]))
                    nc.scalar.activation(Pr[:, p, P:384], Sm[:, p, P:384], ACT.Exp, scale=-1.0,
                                         bias=mn[:, T % 2, 1, h:h + 1],
                                         accum_out=ll[:, T % 2, 1, h:h + 1]).then_inc(exp_ready, 1)
                elif kind == "T":
                    n = number(kind, *a)
                    act.wait_ge(pt_ready, n)
                    if n > 2:
                        act.wait_ge(pv_ready, n - 2)
                    nc.scalar.copy(PT[:, n % 2], ps[:, B_T, 0:384]).then_inc(pt_copied, 1)
                elif kind == "L":
                    T, = a
                    act.wait_ge(sinkarg_ready, T + 1)
                    nc.scalar.activation(es[:, T % 2], es[:, T % 2], ACT.Exp).then_inc(sinkexp_ready, 1)
                elif kind == "aS":
                    act.wait_ge(misc_ready, misc(kind, *a) + 1)
                    line.do(nc.scalar.copy(aSc[0:65, 0:128], ps[0:65, B_M, 0:128]))
                    nc.scalar.copy(aSc[0:64, 128:256], ps[0:64, B_M, 128:256]).then_inc(misc_free, 1)
                elif kind == "aT":
                    act.wait_ge(a_min, 1)
                    nc.scalar.activation(aP[:], ps[:, B_M, 0:KA], ACT.Exp, scale=-1.0, bias=amn,
                                         accum_out=al).then_inc(misc_free, 1)
                    nc.scalar.activation(aes, aes, ACT.Exp).then_inc(a_exp, 1)
                elif kind == "aR":
                    act.wait_ge(misc_ready, misc(kind, *a) + 1)
                    line.do(nc.scalar.copy(aPT[0:65, 0:128], ps[0:65, B_M, 0:128]))
                    nc.scalar.copy(aPT[0:64, 128:256], ps[0:64, B_M, 128:256]).then_inc(misc_free, 1)
                elif kind == "bS":
                    act.wait_ge(misc_ready, misc(kind, *a) + 1)
                    line.do(nc.scalar.copy(bSc[:, 0:32], ps[:, B_M, 0:32]))
                    nc.scalar.copy(bSc[0:65, 32:48], ps[0:65, B_M, 32:48]).then_inc(misc_free, 1)
                elif kind == "bT":
                    u, = a
                    act.wait_ge(misc_free, misc(kind, *a) + 1)
                    nc.scalar.activation(bP[:], bSm[:], ACT.Exp, scale=-1.0, bias=bmn, accum_out=bl).then_inc(b_exp, 1)
                elif kind == "bR":
                    act.wait_ge(misc_ready, misc(kind, *a) + 1)
                    line.do(nc.scalar.copy(bPT[:, 0:32], ps[:, B_M, 0:32]))
                    nc.scalar.copy(bPT[0:65, 32:48], ps[0:65, B_M, 32:48]).then_inc(misc_free, 1)
                elif kind == "N":
                    X, = a
                    act.wait_ge(o_taken, 4 * X + 4)
                    for b in range(2):
                        for c in range(2):
                            k = line.do(nc.scalar.activation(
                                junk, onat[:, b, 512 * c:512 * c + 512].rearrange("p (x y) -> p x y", x=2),
                                ACT.Square, accum_out=ss4[:, b, c:c + 1]))
                            line.need(k)
                    line.step(nc.scalar.activation(ss2, ss4[:, :, 0], ACT.Identity, bias=0.0))
                    for b in range(2):
                        k = line.do(nc.scalar.activation(ss2[:, b:b + 1], ss4[:, b, 1:2], ACT.Identity, bias=ss4[:, b, 0:1]))
                    line.need(k)
                    nc.scalar.activation(rm2, ss2, ACT.Sqrt, bias=eps[:], scale=1.0 / (OT * P)).then_inc(norm_a, 1)
                elif kind == "W":
                    X, j = a
                    act.wait_ge(misc_ready, misc(kind, *a) + 1)
                    dst = oAh[:, j, 0:SEQ] if X == 0 else hh[:, j, 0:SEQ]
                    nc.scalar.activation(dst, ps[:, B_M, 0:SEQ], ACT.Copy,
                                         scale=par[:, C_GOUT + 8 * X + j:C_GOUT + 8 * X + j + 1]).then_inc(oh_ready, 1)
                elif kind == "ND":
                    X, = a
                    act.wait_ge(od_sum, X + 1)
                    nc.scalar.activation(rd[:, 1], rd[:, 0], ACT.Sqrt, bias=eps[:], scale=1.0 / (OT * P)).then_inc(norm_a, 1)
                    act.wait_ge(od_gained, X + 1)
                    dst = oAh[:, :, SEQ:TOK] if X == 0 else hh[:, 0:OT, SEQ:TOK]
                    nc.scalar.copy(dst, od[:, 3]).then_inc(oh_ready, 1)

            act.wait_ge(par_landed, 16)
            for j in range(MT):
                if j % 4 == 0:
                    act.wait_ge(x_landed[j // 4], 16)
                nc.scalar.activation(hh[:, j], xT[:, j], ACT.Copy,
                                     scale=par[:, C_GPM + j:C_GPM + j + 1]).then_inc(xh_ready, 1)
                if j in (3, 7, 11):
                    split(chunk(0, 0, 4, j // 4))
            for n in range(N_ATT):
                split(chunk(0, 0, 4, n + 3))
                for s in PLAN[n]:
                    stage(*s)
            for s in PLAN[N_ATT]:
                stage(*s)

            with act.Fori(0, G_OUT // 2) as i:
                for g in range(2):
                    for j in range(2):
                        split(chunk(B_OUTB, i, 4, 2 * g + j + 3))
                    act.wait_ge(evac_done, i * 2 + (G_IN + G_OUT + g + 1))
                    act.wait_ge(ysq_used, i * 2 + (g + 1))
                    nc.scalar.activation(sq[:], yT[:, bass.ds(i * 4 + 2 * g, 2)], ACT.Square).then_inc(ysq_ready, 1)
            act.wait_ge(sum_ready, 1)
            nc.scalar.activation(rms[:], ps[:, B_M, 0:TOK], ACT.Sqrt, bias=eps[:], scale=1.0 / D_MODEL).then_inc(norm_a, 1)
            for jj in range(MT // 2):
                act.wait_ge(x1_ready, jj + 1)
                for j in (2 * jj, 2 * jj + 1):
                    nc.scalar.activation(hh[:, j], xT[:, j], ACT.Copy,
                                         scale=par[:, C_GPF + j:C_GPF + j + 1]).then_inc(h2h_ready, 1)
                act.wait_ge(ysq_used, SUMS + 1 + jj)
                nc.scalar.activation(sq[:], xT[:, 2 * jj:2 * jj + 2], ACT.Square).then_inc(ysq_ready, 1)

            def ffn_gate(i, first):
                for j in range(4):
                    split(chunk(B_GU, i, 8, j + 3))
                if first:
                    act.wait_ge(sum_ready, 2)
                    nc.scalar.activation(rms[:], ps[:, B_M, 0:TOK], ACT.Sqrt, bias=eps[:],
                                         scale=1.0 / D_MODEL).then_inc(norm_a, 1)
                act.wait_ge(u_ready, i + 1)
                for k in range(2):
                    nc.scalar.activation(cv[:, k], U[:, k, 0:NU - 2], ACT.Identity,
                                         scale=par[:, bass.ds(i * 2 + (C_CW + k), 1)],
                                         bias=par[:, bass.ds(i * 2 + (C_CB + k), 1)]).then_inc(tap_ready, 1)
                split(chunk(B_GU, i, 8, 7))
                act.wait_ge(conv_ready, i + 1)
                line.do(nc.scalar.activation(ge[:, :, 0:SEQ], cv[:, :, 0:SEQ], ACT.Gelu_apprx_tanh))
                nc.scalar.activation(ge[:, :, SEQ:TOK], cv[:, :, SEQ + 2:NU - 2:3], ACT.Gelu_apprx_tanh).then_inc(gelu_ready, 1)
                for j in range(5, 8):
                    split(chunk(B_GU, i, 8, j + 3))
                act.wait_ge(g_ready, i + 1)
                nc.scalar.copy(gh[:, bass.ds(i * 2, 2)], up[:]).then_inc(gh_ready, 1)

            ffn_gate(0, True)
            line.loop(0, 1)
            with act.Fori(0, G_FF - 1) as i:
                line.loop(i, 1)
                ffn_gate(i + 1, False)
            line.end(G_FF - 1)

            for half in range(2):
                with act.Fori(0, FT // 4 - half) as i:
                    for j in range(4):
                        split(chunk(B_DOWN + FT * half, i, 4, j + 3))
                if half == 1:
                    split(chunk(B_DOWN + FT, FT // 4 - 1, 4, 3))
                for m in range(4, 8):
                    if m < 7:
                        act.wait_ge(down_done, 7 * half + m + 1)
                    else:
                        act.wait_ge(weights_used, B_DOWN + FT * (half + 1))
                    nc.scalar.copy(yT[:, 8 * half + m], ps[:, (m + 4) % 8, 0:TOK]).then_inc(down_a, 1)
                act.wait_ge(down_v, 4 * half + 4)
                act.wait_ge(down_a, 4 * half + 4)
                for jj in range(4):
                    act.wait_ge(ysq_used, 2 * SUMS + 1 + 4 * half + jj)
                    nc.scalar.activation(sq[:], yT[:, 8 * half + 2 * jj:8 * half + 2 * jj + 2],
                                         ACT.Square).then_inc(ysq_ready, 1)
            act.wait_ge(sum_ready, 3)
            nc.scalar.activation(rms[:], ps[:, B_M, 0:TOK], ACT.Sqrt, bias=eps[:], scale=1.0 / D_MODEL).then_inc(norm_a, 1)

        @block.vector
        def _(dve):
            line = Line(dve, dve_line)
            V = nc.vector

            def split(c):
                n, slot, _ = c
                dve.wait_ge(hi_ready, n + 1)
                V.tensor_tensor(wl[:, slot], raw[:, slot], wh[:, slot].bitcast(F32), ALU.subtract).then_inc(lo_ready, 1)

            def wide(x, n=2):
                return x.unsqueeze(1).to_broadcast([x.shape[0], n, x.shape[1]])

            def rotate(dst, src, n, scale, signal=None):
                cos, sin = wide(tab[:, T_COS:T_COS + TOK], n), wide(tab[:, T_SIN:T_SIN + TOK], n)
                line.do(V.scalar_tensor_tensor(r1[:, 0:n], src, scale, cos, ALU.mult, ALU.mult))
                line.step(V.stream_shuffle(sh[:, 0:n], src, SWAP))
                line.step(V.scalar_tensor_tensor(r2[:, 0:n], sh[:, 0:n], scale, sin, ALU.mult, ALU.mult))
                return V.tensor_tensor(dst, r1[:, 0:n], r2[:, 0:n], ALU.add)

            def evac(gi):
                dve.wait_ge(weights_used, group_end(gi))
                b = 2 * (gi % 2)
                src = ps[:, b:b + 2, 0:TOK]
                if gi >= G_IN:
                    g = gi - G_IN
                    V.tensor_copy(yT[:, 2 * g:2 * g + 2], src).then_inc(evac_done, 1)
                    return
                kind, t, _ = GROUPS[gi]
                if kind == "kvA":
                    line.step(rotate(kA[:].unsqueeze(1), src[:, 0:1], 1, 1.0))
                    line.do(V.tensor_tensor(vT[:, 0], src[:, 1], rB[:], ALU.mult))
                    line.do(V.tensor_copy(kdup[0:64, 0], kA[0:64]))
                    line.do(V.tensor_copy(kdup[64:128, 0], kA[0:64]))
                    line.do(V.tensor_copy(kdup[0:64, 1], kA[64:128]))
                    V.tensor_copy(kdup[64:128, 1], kA[64:128]).then_inc(evac_done, 1)
                elif kind in ("qA", "qB"):
                    if kind == "qB":
                        T = 4 + t
                        dve.wait_ge(scores_ready, number("S", T - 2, 3))
                        if t >= 2:
                            dve.wait_ge(bq_ready, 2 * (t - 2) + 2)
                        V_last = rotate(qs[:, t % 2], src, 2, -SCALE)
                        V_last.then_inc(evac_done, 1)
                    else:
                        if t >= 2:
                            dve.wait_ge(scores_ready, number("S", t - 2, 3))
                        k = line.do(rotate(qs[:, t % 2], src, 2, -SCALE))
                        line.need(k)
                        kv = t // 2
                        for half in range(2):
                            h0 = 8 * kv + 4 * (t % 2) + half
                            ins = V.tensor_copy(
                                qA[64 * kv:64 * kv + 64, :, h0:h0 + 3:2].rearrange("p s i -> p i s"),
                                qs[64 * half:64 * half + 64, t % 2, :, SEQ:TOK])
                            if half == 0:
                                line.do(ins)
                            else:
                                ins.then_inc(evac_done, 1)
                elif kind == "kB":
                    if t >= 2:
                        dve.wait_ge(scores_ready, number("S", 4 + t - 2, 3))
                        dve.wait_ge(kv_stored[t % 2], 16)
                        dve.wait_ge(bq_ready, 2 * (t - 2) + 2)
                    rotate(ks[:, t % 2], src, 2, 1.0).then_inc(evac_done, 1)
                else:
                    dve.wait_ge(v_stored, 16 * (t + 1))
                    dve.wait_ge(misc_ready, misc("vdec", 3 + t if t else -1) + 1)
                    V.tensor_tensor(vT[:], src, wide(rB[:]), ALU.mult).then_inc(evac_done, 1)

            def stage(kind, *a):
                if kind == "evac":
                    evac(*a)
                elif kind == "ss":
                    dve.wait_ge(misc_free, misc(kind, *a) + 1)
                    dve.wait_ge(misc_ready, misc(kind, *a) + 1)
                    dve.wait_ge(tab_landed, 32)
                    line.step(V.reciprocal(rB[:], rms[:]))
                    line.do(V.tensor_tensor(tab[:, T_COS:T_COS + TOK], tab[:, T_COS:T_COS + TOK], rB[:], ALU.mult))
                    line.do(V.tensor_tensor(tab[:, T_SIN:T_SIN + TOK], tab[:, T_SIN:T_SIN + TOK], rB[:], ALU.mult))
                    line.do(V.memset(qA[:], 0.0))
                    line.step(V.memset(bq[:], 0.0))
                elif kind == "S":
                    T, h = a
                    n = number(kind, *a)
                    p = n % 2
                    dve.wait_ge(scores_ready, n)
                    if n > 2:
                        dve.wait_ge(exp_ready, n - 2)
                    if h == 0 and T >= 2:
                        dve.wait_ge(exp_ready, number("S", T - 2, 3))
                    m = T_MA if T < 4 else T_MB
                    init = sinkn[:, 4 * T + h:4 * T + h + 1] if T < 4 else NEG
                    line.do(V.tensor_tensor_reduce(
                        out=Sm[:, p, 0:P], in0=ps[:, B_S, 0:P], in1=tab[:, m:m + P], scale=1.0, scalar=init,
                        op0=ALU.add, op1=ALU.min, accum_out=mn[:, T % 2, 0, h:h + 1]))
                    V.tensor_tensor_reduce(
                        out=Sm[:, p, P:384], in0=ps[:, B_S, P:384], in1=tab[:, m + P:m + 384], scale=1.0, scalar=init,
                        op0=ALU.add, op1=ALU.min, accum_out=mn[:, T % 2, 1, h:h + 1]).then_inc(masked_ready, 1)
                elif kind == "L":
                    T, = a
                    dve.wait_ge(masked_ready, number("S", T, 3))
                    sk = par[:, C_SINK + 4 * T:C_SINK + 4 * T + 4]
                    V.tensor_tensor(es[:, T % 2], mn[:, T % 2], wide(sk), ALU.add).then_inc(sinkarg_ready, 1)
                elif kind == "O":
                    T, = a
                    dve.wait_ge(pv_ready, number("V", T, 3))
                    dve.wait_ge(exp_ready, number("S", T, 3))
                    if T == 4:
                        dve.wait_ge(misc_ready, misc("W", 0, OT - 1) + 1)
                    if T < 4:
                        dve.wait_ge(sinkexp_ready, T + 1)
                        line.step(V.tensor_tensor(ll[:, T % 2], ll[:, T % 2], es[:, T % 2], ALU.add))
                    line.step(V.reciprocal(rl[:, T % 2], ll[:, T % 2]))
                    c = 256 * (T % 4)
                    for b in range(2):
                        ins = V.tensor_tensor(
                            onat[:, b, c:c + 256].rearrange("p (a e) -> p a e", a=4),
                            ps[:, B_O, 256 * b:256 * b + 256].rearrange("p (a e) -> p a e", a=4),
                            rl[:, T % 2, b].unsqueeze(2).to_broadcast([P, 4, HD]), ALU.mult)
                        if b == 0:
                            line.do(ins)
                        else:
                            ins.then_inc(o_taken, 1)
                elif kind == "aS":
                    dve.wait_ge(KtA_landed, 16)
                elif kind == "aT":
                    dve.wait_ge(misc_ready, misc(kind, *a) + 1)
                    line.step(V.tensor_reduce(amn, ps[:, B_M, 0:KA], AX.X, ALU.min))
                    line.step(V.tensor_tensor(amn, amn, sinkn[:, H_A:H_A + 1], ALU.min))
                    V.tensor_tensor(aes, amn, par[:, C_SROW:C_SROW + 1], ALU.add).then_inc(a_min, 1)
                    dve.wait_ge(a_exp, 1)
                    line.step(V.tensor_tensor(al, al, aes, ALU.add))
                    line.step(V.reciprocal(ari, al))
                    V.tensor_scalar(aP[:], aP[:], ari, None, ALU.mult).then_inc(a_p, 1)
                elif kind == "aV":
                    dve.wait_ge(misc_ready, misc(kind, *a) + 1)
                    o = ps[:, B_M, 0:P].rearrange("p (s h) -> p s h", h=H_A)
                    for kv in range(2):
                        for half in range(2):
                            ins = V.tensor_copy(
                                od[64 * half:64 * half + 64, 0, 4 * kv:4 * kv + 4, :].rearrange("p i s -> p s i"),
                                o[64 * kv:64 * kv + 64, :, 8 * kv + half:8 * kv + 8:2])
                            if (kv, half) == (1, 1):
                                ins.then_inc(misc_free, 1)
                            else:
                                line.do(ins)
                elif kind == "bQ":
                    u, = a
                    t, hp = u // 2, u % 2
                    dve.wait_ge(evac_done, GI[("kB", t)] + 1)
                    dve.wait_ge(Kd_landed[u % 2], 16 * (u // 2 + 1))
                    if u >= 2:
                        dve.wait_ge(misc_ready, misc("bS", u - 2) + 1)
                    line.do(V.tensor_copy(Kd[:, u % 2, :, KEYS_B], ks[:, t % 2, hp, SEQ:TOK]))
                    line.do(V.tensor_copy(bq[0:64, u % 2, :, 0], qs[0:64, t % 2, hp, SEQ:TOK]))
                    V.tensor_copy(bq[64:128, u % 2, :, 1], qs[64:128, t % 2, hp, SEQ:TOK]).then_inc(bq_ready, 1)
                elif kind == "bT":
                    u, = a
                    dve.wait_ge(misc_ready, misc(kind, *a) + 1)
                    V.tensor_tensor_reduce(
                        out=bSm[:], in0=ps[0:16, B_M, 0:KB], in1=tab[0:16, T_MD:T_MD + KB], scale=1.0, scalar=NEG,
                        op0=ALU.add, op1=ALU.min, accum_out=bmn).then_inc(misc_free, 1)
                    dve.wait_ge(b_exp, u + 1)
                    line.step(V.reciprocal(bri, bl))
                    V.tensor_scalar(bP[:], bP[:], bri, None, ALU.mult).then_inc(b_p, 1)
                elif kind == "bV":
                    u, = a
                    dve.wait_ge(misc_ready, misc(kind, *a) + 1)
                    o = ps[:, B_M, 0:16].rearrange("p (s h) -> p s h", h=2)
                    line.do(V.tensor_copy(od[0:64, 0, u], o[0:64, :, 0]))
                    V.tensor_copy(od[64:128, 0, u], o[64:128, :, 1]).then_inc(misc_free, 1)
                elif kind == "N":
                    X, = a
                    dve.wait_ge(norm_a, 2 * X + 1)
                    line.step(V.reciprocal(ri2, rm2))
                    for b in range(2):
                        ins = V.tensor_scalar(onat[:, b], onat[:, b], ri2[:, b:b + 1], None, ALU.mult)
                        if b == 0:
                            line.do(ins)
                        else:
                            ins.then_inc(onat_scaled, 1)
                elif kind == "W":
                    X, j = a
                    dve.wait_ge(oh_ready, number_oh(kind, *a))
                    hi = oAh[:, j, 0:SEQ] if X == 0 else hh[:, j, 0:SEQ]
                    lo = oAl[:, j, 0:SEQ] if X == 0 else hh[:, OT + j, 0:SEQ]
                    V.scalar_tensor_tensor(lo, ps[:, B_M, 0:SEQ], par[:, C_GOUT + 8 * X + j:C_GOUT + 8 * X + j + 1],
                                           hi.bitcast(F32), ALU.mult, ALU.subtract).then_inc(misc_free, 1)
                elif kind == "ND":
                    X, = a
                    dve.wait_ge(misc_free, misc("aV") + 1 if X == 0 else misc("bV", 7) + 1)
                    V.tensor_tensor(od[:, 1], od[:, 0], od[:, 0], ALU.mult).then_inc(od_sq, 1)
                    dve.wait_ge(misc_ready, misc(kind, *a) + 1)
                    V.tensor_reduce(rd[:, 0], ps[:, B_M, 0:OT * NDEC].rearrange("p (j s) -> p s j", s=NDEC),
                                    AX.X, ALU.add).then_inc(od_sum, 1)
                    dve.wait_ge(norm_a, 2 * X + 2)
                    line.step(V.reciprocal(rd[:, 2], rd[:, 1]))
                    line.step(V.tensor_tensor(od[:, 2], od[:, 0], wide(rd[:, 2], OT), ALU.mult))
                    g = par[:, C_GOUT + 8 * X:C_GOUT + 8 * X + 8].unsqueeze(2).to_broadcast([P, OT, NDEC])
                    V.tensor_tensor(od[:, 3], od[:, 2], g, ALU.mult).then_inc(od_gained, 1)
                    dve.wait_ge(oh_ready, number_oh(kind, *a))
                    dve.wait_ge(od_gained, X + 1)
                    hi = oAh[:, :, SEQ:TOK] if X == 0 else hh[:, 0:OT, SEQ:TOK]
                    lo = oAl[:, :, SEQ:TOK] if X == 0 else hh[:, OT:2 * OT, SEQ:TOK]
                    V.tensor_tensor(lo, od[:, 3], hi.bitcast(F32), ALU.subtract).then_inc(misc_free, 1)

            dve.wait_ge(par_landed, 16)
            V.memset(eps[:], EPS).then_inc(const_ready, 1)
            line.do(V.tensor_scalar(sinkn, par[:, C_SINK:C_SINK + H_A + 1], -1.0, None, ALU.mult))
            V.memset(ones[:], 1.0).then_inc(const_ready, 1)
            for j in range(MT):
                dve.wait_ge(xh_ready, j + 1)
                V.scalar_tensor_tensor(hl[:, j], xT[:, j], par[:, C_GPM + j:C_GPM + j + 1],
                                       hh[:, j].bitcast(F32), ALU.mult, ALU.subtract).then_inc(xl_ready, 1)
                if j in (3, 7):
                    split(chunk(0, 0, 4, j // 4))
            for n in range(N_ATT):
                split(chunk(0, 0, 4, n + 2))
                for s in PLAN[n]:
                    stage(*s)
            for s in PLAN[N_ATT]:
                stage(*s)

            with dve.Fori(0, G_OUT // 2) as i:
                for g in range(2):
                    for j in range(2):
                        split(chunk(B_OUTB, i, 4, 2 * g + j + 2))
                    dve.wait_ge(weights_used, i * 4 + (B_OUTB + 2 * g + 2))
                    b = 2 * ((G_IN + G_OUT + g) % 2)
                    y2 = yT[:, bass.ds(i * 4 + 2 * g, 2)]
                    V.tensor_tensor(y2, ps[:, b:b + 2, 0:TOK], y2, ALU.add).then_inc(evac_done, 1)
            dve.wait_ge(norm_a, 5)
            V.reciprocal(rB[:], rms[:]).then_inc(rB_ready, 1)
            dve.wait_ge(rB_ready, 1)

            def low(jj):
                for j in (2 * jj, 2 * jj + 1):
                    dve.wait_ge(h2h_ready, j + 1)
                    V.scalar_tensor_tensor(hl[:, j], xT[:, j], par[:, C_GPF + j:C_GPF + j + 1],
                                           hh[:, j].bitcast(F32), ALU.mult, ALU.subtract).then_inc(h2l_ready, 1)

            for jj in range(MT // 2):
                y2 = yT[:, 2 * jj:2 * jj + 2]
                line.step(V.tensor_tensor(y2, y2, wide(rB[:]), ALU.mult))
                for j in (2 * jj, 2 * jj + 1):
                    ins = V.scalar_tensor_tensor(xT[:, j], yT[:, j], par[:, C_GQM + j:C_GQM + j + 1], xT[:, j],
                                                 ALU.mult, ALU.add)
                    if j % 2 == 0:
                        line.do(ins)
                    else:
                        ins.then_inc(x1_ready, 1)
                if jj:
                    low(jj - 1)
            low(MT // 2 - 1)

            def ffn(i, first):
                for j in range(4):
                    split(chunk(B_GU, i, 8, j + 2))
                if first:
                    dve.wait_ge(norm_a, 6)
                    V.reciprocal(rB[:], rms[:]).then_inc(rB_ready, 1)
                    dve.wait_ge(rB_ready, 2)
                dve.wait_ge(weights_used, i * 8 + (B_GU + 4))
                dve.wait_ge(state_ready, i + 1)
                line.do(V.tensor_tensor(U[:, :, 2:2 + SEQ], ps[:, 0:2, 0:SEQ], wide(rB[:, 0:SEQ]), ALU.mult))
                V.tensor_tensor(U_dec[:, :, :, 2], ps[:, 0:2, SEQ:TOK], wide(rB[:, SEQ:TOK]), ALU.mult).then_inc(u_ready, 1)
                split(chunk(B_GU, i, 8, 6))
                dve.wait_ge(tap_ready, i * 2 + 2)
                for tap in (1, 2):
                    for k in range(2):
                        ins = V.scalar_tensor_tensor(
                            cv[:, k], U[:, k, tap:tap + NU - 2],
                            par[:, bass.ds(i * 2 + (C_CW + FT * tap + k), 1)], cv[:, k], ALU.mult, ALU.add)
                        if (tap, k) == (2, 1):
                            ins.then_inc(conv_ready, 1)
                        else:
                            n = line.do(ins)
                    if tap == 1:
                        line.need(n)
                for j in range(5, 8):
                    split(chunk(B_GU, i, 8, j + 2))
                dve.wait_ge(weights_used, i * 8 + (B_GU + 8))
                V.tensor_tensor(up[:], ps[:, 2:4, 0:TOK], wide(rB[:]), ALU.mult).then_inc(up_taken, 1)
                dve.wait_ge(up_taken, i + 1)
                dve.wait_ge(gelu_ready, i + 1)
                V.tensor_tensor(up[:], up[:], ge[:], ALU.mult).then_inc(g_ready, 1)
                dve.wait_ge(g_ready, i + 1)
                dve.wait_ge(gh_ready, i + 1)
                V.tensor_tensor(gl[:, bass.ds(i * 2, 2)], up[:], gh[:, bass.ds(i * 2, 2)].bitcast(F32),
                                ALU.subtract).then_inc(gl_ready, 1)

            ffn(0, True)
            with dve.Fori(0, G_FF - 1) as i:
                line.loop(i, 4)
                ffn(i + 1, False)
            line.end(G_FF - 1)

            for half in range(2):
                with dve.Fori(0, FT // 4 - half) as i:
                    for j in range(4):
                        split(chunk(B_DOWN + FT * half, i, 4, j + 2))
                if half == 1:
                    for j in range(2):
                        split(chunk(B_DOWN + FT, FT // 4 - 1, 4, j + 2))
                for m in range(4):
                    dve.wait_ge(down_done, 7 * half + m + 1)
                    V.tensor_copy(yT[:, 8 * half + m], ps[:, (m + 4) % 8, 0:TOK]).then_inc(down_v, 1)
            dve.wait_ge(norm_a, 7)
            V.reciprocal(rB[:], rms[:]).then_inc(rB_ready, 1)
            dve.wait_ge(rB_ready, 3)
            for jj in range(MT // 2):
                y2 = yT[:, 2 * jj:2 * jj + 2]
                line.step(V.tensor_tensor(y2, y2, wide(rB[:]), ALU.mult))
                for j in (2 * jj, 2 * jj + 1):
                    ins = V.scalar_tensor_tensor(yT[:, j], yT[:, j], par[:, C_GQF + j:C_GQF + j + 1], xT[:, j],
                                                 ALU.mult, ALU.add)
                    if j % 4 == 3:
                        ins.then_inc(out_ready, 1)
                    else:
                        line.do(ins)

        @block.gpsimd
        def _(pool):
            line = Line(pool, pool_line)
            G = nc.gpsimd

            def load_K(u):
                if u >= 2:
                    pool.wait_ge(misc_ready, misc("bS", u - 2) + 1)
                G.dma_start(Kd[:, u % 2], d["kb"][u]).then_inc(Kd_landed[u % 2], 16)

            def load_V(u):
                if u:
                    pool.wait_ge(misc_ready, misc("bV", u - 1) + 1)
                    pool.wait_ge(Vd_full, 16 * u)
                G.dma_start(Vd[:, 0:2], d["vb"][u, :, 0:2]).then_inc(Vd_landed, 16)
                G.dma_start(Vd[0:64, 2], d["vb"][u, 0:64, 2]).then_inc(Vd_landed, 16)

            def self_V(u):
                pool.wait_ge(Vd_landed, 32 * (u + 1))
                pool.wait_ge(misc_free, misc("vdec", 4 + u // 2) + 1)
                G.dma_start(Vd[64:65, 2], vdec[:, P * (u % 2):P * (u % 2) + P]).then_inc(Vd_full, 16)

            def stage(kind, *a):
                if kind == "ss":
                    pool.wait_ge(misc_ready, misc("ss") + 1)
                    G.dma_start(KtA[:], d["ka"]).then_inc(KtA_landed, 16)
                    G.dma_start(VtA[0:64], d["va"]).then_inc(VtA_landed, 16)
                elif kind == "evac":
                    gi, = a
                    if gi >= G_IN:
                        return
                    what, t, _ = GROUPS[gi]
                    if what == "kvA":
                        pool.wait_ge(evac_done, gi + 1)
                        pool.wait_ge(KtA_landed, 16)
                        G.tensor_copy(KtA[:, :, 64], kA[:, SEQ:TOK]).then_inc(aq_ready, 1)
                        G.dma_start(d["out_ka"], kA[:]).then_inc(other_stored, 16)
                        G.dma_start(d["out_va"], vT[:, 0]).then_inc(v_stored, 16)
                    elif what == "kB":
                        pool.wait_ge(evac_done, gi + 1)
                        G.dma_start(d["out_kb"][t], ks[:, t % 2]).then_inc(kv_stored[t % 2], 16)
                    elif what == "vB":
                        pool.wait_ge(evac_done, gi + 1)
                        G.dma_start(d["out_vb"][t], vT[:]).then_inc(v_stored, 16)
                elif kind == "vdec":
                    T, = a
                    if T < 0:
                        pool.wait_ge(VtA_landed, 16)
                        pool.wait_ge(misc_free, misc("vdec", -1) + 1)
                        G.dma_start(VtA[64:65, 0], vdec[:, 0:P]).then_inc(VtA_full, 16)
                    else:
                        self_V(2 * (T - 4))
                elif kind == "aV":
                    pool.wait_ge(misc_ready, misc("aV") + 1)
                    load_K(0)
                    load_K(1)
                    load_V(0)
                elif kind == "bS" and a[0] + 2 < 8:
                    load_K(a[0] + 2)
                elif kind == "bV" and a[0] + 1 < 8:
                    load_V(a[0] + 1)
                    if a[0] % 2 == 0:
                        self_V(a[0] + 1)

            for c in range(4):
                pool.wait_ge(x_landed[c], 16)
                G.tensor_tensor(xsq[:, 4 * c:4 * c + 4], xT[:, 4 * c:4 * c + 4], xT[:, 4 * c:4 * c + 4],
                                ALU.mult).then_inc(xsq_ready, 1)
            for n in range(N_ATT + 1):
                for s in PLAN[n]:
                    stage(*s)

            def clear_squares():
                G.memset(sqa[:], 0.0).then_inc(ysq_used, 1)

            def add_squares(c, k):
                pool.wait_ge(ysq_ready, k + (8 * c + 1))
                pool.wait_ge(ysq_used, k + (SUMS * c + 1))
                G.tensor_tensor(sqa[:], sqa[:], sq[:], ALU.add).then_inc(ysq_used, 1)

            pool.wait_ge(misc_free, len(MISC))
            clear_squares()
            with pool.Fori(0, G_OUT) as i:
                add_squares(0, i)
            pool.wait_ge(sum_ready, 1)
            clear_squares()
            for jj in range(MT // 2):
                add_squares(1, jj)
            pool.wait_ge(sum_ready, 2)
            line.step(G.memset(U[:], 0.0))

            def window(i):
                if not isinstance(i, int) or i > 0:
                    pool.wait_ge(conv_ready, i)
                    pool.wait_ge(u_kept, i)
                G.tensor_copy(U_dec[:, :, :, 0:2],
                              par[:, bass.ds(i * (32) + C_ST, 32)].rearrange("p (k s c) -> p k s c", k=2, c=2)
                              ).then_inc(state_ready, 1)
                pool.wait_ge(u_ready, i + 1)
                line.do(G.tensor_copy(co[:, bass.ds(i * 2, 2), 0:2], U[:, :, SEQ:SEQ + 2]))
                G.tensor_copy(co[:, bass.ds(i * 2, 2), 2:2 + 2 * NDEC].rearrange("p k (s c) -> p k s c", c=2),
                              U_dec[:, :, :, 1:3]).then_inc(u_kept, 1)

            window(0)
            with pool.Fori(0, G_FF - 1) as i:
                window(i + 1)
            pool.wait_ge(u_kept, G_FF)
            G.dma_start(d["out_conv"], co[:]).then_inc(other_stored, 16)
            pool.wait_ge(gl_ready, G_FF)
            clear_squares()
            for jj in range(MT // 2):
                add_squares(2, jj)
            pool.wait_ge(other_stored, 32)
            pool.wait_ge(kv_stored[0], 32)
            pool.wait_ge(kv_stored[1], 32)
            pool.wait_ge(v_stored, 16 * 5)

        @block.tensor
        def _(pe):
            def mm3(out, w, x, xl, start, stop):
                slot, c = w
                a, b = wh[:, slot, c:c + P], wl[:, slot, c:c + P]
                nc.tensor.matmul(out, a, x, start=start, stop=False)
                nc.tensor.matmul(out, a, xl, start=False, stop=False)
                return nc.tensor.matmul(out, b, x, start=False, stop=stop)

            def gemm(c, bank, xh, xl, kt0, first, last):
                n, slot, _ = c
                pe.wait_ge(lo_ready, n + 1)
                for k in range(4):
                    for m in range(2):
                        ins = mm3(ps[:, bank + m, 0:TOK], (slot, 256 * k + P * m), xh[:, kt0 + k], xl[:, kt0 + k],
                                  first and k == 0, last and k == 3)
                ins.then_inc(weights_used, 1)
                return ins

            def take_misc(kind, *a):
                n = misc(kind, *a)
                if n:
                    pe.wait_ge(misc_free, n)

            def stage(kind, *a):
                if kind == "ss":
                    pe.wait_ge(const_ready, 2)
                    for j in range(MT):
                        if j % 4 == 0:
                            pe.wait_ge(xsq_ready, j // 4 + 1)
                        ins = nc.tensor.matmul(ps[:, B_M, 0:TOK], ones[:], xsq[:, j], start=j == 0, stop=j == MT - 1)
                    ins.then_inc(misc_ready, 1)
                elif kind == "vtr":
                    T, = a
                    pe.wait_ge(tab_landed, 32)
                    pe.wait_ge(evac_done, (GI[("kvA", 0)] if T < 0 else GI[("vB", T - 4)]) + 1)
                    take_misc(kind, *a)
                    w = 1 if T < 0 else 2
                    for b in range(2):
                        for m in range(w):
                            ins = nc.tensor.transpose(ps[:, B_M, (b * w + m) * P:(b * w + m + 1) * P],
                                                      vT[:, m, P * b:P * b + P], ident[:])
                    ins.then_inc(misc_ready, 1)
                elif kind == "vdec":
                    T, = a
                    take_misc(kind, *a)
                    for m in range(1 if T < 0 else 2):
                        ins = nc.tensor.transpose(ps[0:NDEC, B_M, P * m:P * m + P], vT[:, m, SEQ:TOK], ident[:])
                    ins.then_inc(misc_ready, 1)
                elif kind == "S":
                    T, h = a
                    n = number(kind, *a)
                    pe.wait_ge(evac_done, (q_group(T) if T < 4 else GI[("kB", T - 4)]) + 1)
                    if n > 1:
                        pe.wait_ge(masked_ready, n - 1)
                    half, m = heads_of(T, h)
                    q = qs[half, T % 2, m]
                    k = kdup[half, T // 2] if T < 4 else ks[half, T % 2, m]
                    nc.tensor.matmul(ps[:, B_S, 0:P], q[:, 0:P], k[:, 0:P], start=True, stop=True)
                    nc.tensor.matmul(ps[:, B_S, P:384], q[:, P:SEQ], k[:, 0:SEQ], start=True,
                                     stop=True).then_inc(scores_ready, 1)
                elif kind == "T":
                    n = number(kind, *a)
                    pe.wait_ge(exp_ready, n)
                    if n > 1:
                        pe.wait_ge(pt_copied, n - 1)
                    for c in range(3):
                        ins = nc.tensor.transpose(ps[:, B_T, P * c:P * c + P], Pr[:, n % 2, P * c:P * c + P], ident[:])
                    ins.then_inc(pt_ready, 1)
                elif kind == "V":
                    T, h = a
                    n = number(kind, *a)
                    pe.wait_ge(pt_copied, n)
                    if h == 0:
                        pe.wait_ge(misc_free, misc("vtr", T if T >= 4 else -1) + 1)
                        if T:
                            pe.wait_ge(o_taken, T)
                    if T < 4:
                        v = [vnA[:, b, HD * (T // 2):HD * (T // 2) + HD] for b in range(2)]
                    else:
                        v = [vn[:, T % 2, b, HD * h:HD * h + HD] for b in range(2)]
                    o = [ps[:, B_O, 256 * b + HD * h:256 * b + HD * h + HD] for b in range(2)]
                    pt = PT[:, n % 2]
                    nc.tensor.matmul(o[0], pt[:, 0:P], v[0], start=True, stop=True)
                    nc.tensor.matmul(o[1], pt[:, P:2 * P], v[0], start=True, stop=False)
                    nc.tensor.matmul(o[1], pt[:, 2 * P:384], v[1], start=False, stop=True).then_inc(pv_ready, 1)
                elif kind == "aS":
                    pe.wait_ge(evac_done, GI[("qA", 3)] + 1)
                    pe.wait_ge(aq_ready, 1)
                    take_misc(kind, *a)
                    for c, (k0, k1) in enumerate(KSPLIT_A):
                        for s in range(NDEC):
                            ins = nc.tensor.matmul(ps[0:k1 - k0, B_M, P * c + H_A * s:P * c + H_A * s + H_A],
                                                   KtA[:, s, k0:k1], qA[:, s], start=True, stop=True)
                    ins.then_inc(misc_ready, 1)
                elif kind == "aT":
                    take_misc(kind, *a)
                    for c, (k0, k1) in enumerate(KSPLIT_A):
                        ins = nc.tensor.transpose(ps[:, B_M, k0:k1], aSc[0:k1 - k0, P * c:P * c + P],
                                                  ident[0:k1 - k0, 0:k1 - k0])
                    ins.then_inc(misc_ready, 1)
                elif kind == "aR":
                    pe.wait_ge(a_p, 1)
                    take_misc(kind, *a)
                    for c, (k0, k1) in enumerate(KSPLIT_A):
                        ins = nc.tensor.transpose(ps[0:k1 - k0, B_M, P * c:P * c + P], aP[:, k0:k1], ident[:])
                    ins.then_inc(misc_ready, 1)
                elif kind == "aV":
                    pe.wait_ge(VtA_full, 16)
                    take_misc(kind, *a)
                    for s in range(NDEC):
                        for c, (k0, k1) in enumerate(KSPLIT_A):
                            ins = nc.tensor.matmul(ps[:, B_M, H_A * s:H_A * s + H_A], VtA[0:k1 - k0, c, s],
                                                   aPT[0:k1 - k0, P * c + H_A * s:P * c + H_A * s + H_A],
                                                   start=c == 0, stop=c == 1)
                    ins.then_inc(misc_ready, 1)
                elif kind == "bS":
                    u, = a
                    pe.wait_ge(bq_ready, u + 1)
                    take_misc(kind, *a)
                    for c, (k0, k1) in enumerate(KSPLIT_B):
                        for s in range(NDEC):
                            ins = nc.tensor.matmul(ps[0:k1 - k0, B_M, 16 * c + 2 * s:16 * c + 2 * s + 2],
                                                   Kd[:, u % 2, s, k0:k1], bq[:, u % 2, s], start=True, stop=True)
                    ins.then_inc(misc_ready, 1)
                elif kind == "bT":
                    take_misc(kind, *a)
                    for c, (k0, k1) in enumerate(KSPLIT_B):
                        ins = nc.tensor.transpose(ps[0:16, B_M, k0:k1], bSc[0:k1 - k0, 16 * c:16 * c + 16],
                                                  ident[0:k1 - k0, 0:k1 - k0])
                    ins.then_inc(misc_ready, 1)
                elif kind == "bR":
                    u, = a
                    pe.wait_ge(b_p, u + 1)
                    take_misc(kind, *a)
                    for c, (k0, k1) in enumerate(KSPLIT_B):
                        ins = nc.tensor.transpose(ps[0:k1 - k0, B_M, 16 * c:16 * c + 16], bP[:, k0:k1],
                                                  ident[0:16, 0:16])
                    ins.then_inc(misc_ready, 1)
                elif kind == "bV":
                    u, = a
                    pe.wait_ge(Vd_full, 16 * (u + 1))
                    take_misc(kind, *a)
                    for s in range(NDEC):
                        for c, (k0, k1) in enumerate(KSPLIT_B):
                            ins = nc.tensor.matmul(ps[:, B_M, 2 * s:2 * s + 2], Vd[0:k1 - k0, c, s],
                                                   bPT[0:k1 - k0, 16 * c + 2 * s:16 * c + 2 * s + 2],
                                                   start=c == 0, stop=c == 2)
                    ins.then_inc(misc_ready, 1)
                elif kind == "W":
                    X, j = a
                    pe.wait_ge(onat_scaled, X + 1)
                    take_misc(kind, *a)
                    for b in range(2):
                        ins = nc.tensor.transpose(ps[:, B_M, P * b:P * b + P], onat[:, b, P * j:P * j + P], ident[:])
                    ins.then_inc(misc_ready, 1)
                elif kind == "ND":
                    X, = a
                    pe.wait_ge(od_sq, X + 1)
                    take_misc(kind, *a)
                    nc.tensor.matmul(ps[:, B_M, 0:OT * NDEC], ones[:], od[:, 1].rearrange("p j s -> p (j s)"),
                                     start=True, stop=True).then_inc(misc_ready, 1)

            def sum_squares(signal):
                for k in range(2):
                    ins = nc.tensor.matmul(ps[:, B_M, 0:TOK], ones[:], sqa[:, k], start=k == 0, stop=k == 1)
                ins.then_inc(signal, 1)

            for n in range(N_ATT):
                if n < N_IN:
                    gi, c = n // 4, n % 4
                    if c == 0 and gi >= 2:
                        pe.wait_ge(evac_done, gi - 1)
                    if gi == 0:
                        pe.wait_ge(xl_ready, 4 * c + 4)
                    gemm(chunk(0, 0, 4, n), 2 * (gi % 2), hh, hl, 4 * c, c == 0, c == 3)
                else:
                    g, c = (n - N_IN) // 2, (n - N_IN) % 2
                    gi = G_IN + g
                    if c == 0:
                        pe.wait_ge(evac_done, gi - 1)
                    if n == N_IN:
                        pe.wait_ge(misc_free, misc("ND", 0) + 1)
                    gemm(chunk(0, 0, 4, n), 2 * (gi % 2), oAh, oAl, 4 * c, c == 0, c == 1)
                for s in PLAN[n]:
                    stage(*s)
            for s in PLAN[N_ATT]:
                stage(*s)

            pe.wait_ge(misc_free, len(MISC))
            with pe.Fori(0, G_OUT // 2) as i:
                for g in range(2):
                    pe.wait_ge(evac_done, i * 2 + (G_IN + G_OUT + g - 1))
                    for c in range(2):
                        gemm(chunk(B_OUTB, i, 4, 2 * g + c), 2 * ((G_IN + G_OUT + g) % 2), hh, hh[:, OT:2 * OT],
                             4 * c, c == 0, c == 1)
            pe.wait_ge(ysq_used, SUMS)
            sum_squares(sum_ready)

            def ffn(i, first):
                if not first:
                    pe.wait_ge(u_ready, i)
                for c in range(4):
                    if first:
                        pe.wait_ge(h2l_ready, 4 * c + 4)
                    gemm(chunk(B_GU, i, 8, c), 0, hh, hl, 4 * c, c == 0, c == 3)
                if first:
                    pe.wait_ge(ysq_used, 2 * SUMS)
                    sum_squares(sum_ready)
                if not first:
                    pe.wait_ge(up_taken, i)
                for c in range(4):
                    gemm(chunk(B_GU, i, 8, 4 + c), 2, hh, hl, 4 * c, c == 0, c == 3)

            ffn(0, True)
            with pe.Fori(0, G_FF - 1) as i:
                ffn(i + 1, False)

            def down(c, kt, first, last, half):
                n, slot, _ = c
                pe.wait_ge(lo_ready, n + 1)
                for m in range(8):
                    if first and half == 0 and m == 4:
                        pe.wait_ge(u_ready, G_FF)
                    if first and half == 0 and m == 6:
                        pe.wait_ge(up_taken, G_FF)
                    if first and half == 1:
                        if m < 4:
                            pe.wait_ge(down_v, m + 1)
                        else:
                            pe.wait_ge(down_a, m - 3)
                    ins = mm3(ps[:, (m + 4) % 8, 0:TOK], (slot, P * m), gh[:, kt], gl[:, kt], first, last)
                    if last and m < 7:
                        ins.then_inc(down_done, 1)
                ins.then_inc(weights_used, 1)

            for half in range(2):
                base = B_DOWN + FT * half
                for j in range(4):
                    if half == 0 and j % 2 == 0:
                        pe.wait_ge(gl_ready, j // 2 + 1)
                    down(chunk(base, 0, 4, j), j, j == 0, False, half)
                with pe.Fori(0, FT // 4 - 2) as i:
                    if half == 0:
                        pe.wait_ge(gl_ready, i * 2 + 4)
                    for j in range(4):
                        down(chunk(base + 4, i, 4, j), i * 4 + (4 + j), False, False, half)
                if half == 0:
                    pe.wait_ge(gl_ready, G_FF)
                for j in range(4):
                    down(chunk(base, FT // 4 - 1, 4, j), FT - 4 + j, False, j == 3, half)
            pe.wait_ge(ysq_used, 3 * SUMS)
            sum_squares(sum_ready)


def shape_tables():
    tab = np.zeros((P, N_TAB), np.float32)
    q = np.arange(P)[:, None]

    def count(dist):
        return sum(((dist >= 0) & (dist <= w) & (dist % s == 0)).astype(int) for w, s in DILATIONS)

    def cost(c):
        return np.where(c > 0, -np.log(np.maximum(c, 1)), NEG).astype(np.float32)

    dist = np.concatenate([q - np.arange(P)[None], P + q - np.arange(2 * P)[None]], axis=1)
    tab[:, T_MA:T_MA + 384] = cost(((dist >= 0) & (dist <= WINDOW_A)).astype(int))
    tab[:, T_MB:T_MB + 384] = cost(count(dist))
    tab[:, T_MD:T_MD + KB] = cost(count(np.concatenate([rows_b_dist(), [0]])))[None]
    half = ROT // 2
    inv = np.float32(THETA) ** (-np.arange(half, dtype=np.float32) * np.float32(2.0 / ROT))
    pos = np.concatenate([np.arange(SEQ), np.full(NDEC, PAST)]).astype(np.float32)
    ang = (pos[:, None] * inv[None]).astype(np.float32).astype(np.float64)
    cos, sin = np.cos(ang).T.astype(np.float32), np.sin(ang).T.astype(np.float32)
    for o in (0, HD):
        tab[o:o + HD, T_COS:T_COS + TOK] = 1.0
        tab[o:o + half, T_COS:T_COS + TOK] = cos
        tab[o + half:o + ROT, T_COS:T_COS + TOK] = cos
        tab[o:o + half, T_SIN:T_SIN + TOK] = -sin
        tab[o + half:o + ROT, T_SIN:T_SIN + TOK] = sin
    return tab


def rows_b_dist():
    dist = set()
    for w, s in DILATIONS:
        dist |= set(range(s, w + 1, s))
    return np.array(sorted(dist, reverse=True))


def kernel(**inputs):
    import concourse.bacc as bacc
    from concourse.bass_utils import run_bass_kernel_spmd

    v = {k: np.asarray(a) for k, a in inputs.items()}
    asc = np.ascontiguousarray

    def cols(a, n):
        return np.reshape(a, (n, P)).T

    x = np.concatenate([v["x_prompt"][0], v["x_sample"][:, 0]], axis=0)
    arrays = {
        "x": asc(x.T.reshape(MT, P, TOK).transpose(1, 0, 2)),
        "ident": np.eye(P, dtype=np.float32),
        "tab": shape_tables(),
    }
    st = v["state_conv"][0].transpose(2, 0, 1).reshape(FT, P, NDEC, 2).transpose(1, 0, 2, 3)
    sinks = v["attn_sinks"][0].reshape(H_A)
    arrays["par"] = asc(np.concatenate([
        cols(v["g_pre_mix"][0], MT), cols(v["g_post_mix"][0], MT), cols(v["g_pre_ffn"][0], MT),
        cols(v["g_post_ffn"][0], MT), cols(v["g_out_a"][0], OT), cols(v["g_out_b"][0], OT),
        *[cols(v["conv_w"][0, j], FT) for j in range(3)], cols(v["conv_b"][0], FT),
        st.reshape(P, FT * 2 * NDEC), np.broadcast_to(sinks, (P, H_A)), np.tile(sinks, NDEC)[:, None],
    ], axis=1))
    w = v["w_in"][0].reshape(4, 4, P, G_IN, 256)
    arrays["w_in"] = asc(w.transpose(3, 0, 2, 1, 4)).reshape(G_IN, 4, P, CH)
    w = v["w_out"][0].reshape(2, 2, 4, P, G_OUT, 256)
    arrays["w_out"] = asc(w.transpose(0, 4, 1, 3, 2, 5)).reshape(4 * G_OUT, P, CH)
    for n in ("w_gate", "w_up"):
        w = v[n][0].reshape(4, 4, P, G_FF, 256)
        arrays[n] = asc(w.transpose(3, 0, 2, 1, 4)).reshape(4 * G_FF, P, CH)
    w = v["w_down"][0].reshape(FT, P, 2, CH)
    arrays["w_down"] = asc(w.transpose(2, 0, 1, 3)).reshape(2 * FT, P, CH)
    k = v["cache_a_k"][0].reshape(NDEC, WINDOW_A, P).transpose(2, 0, 1)
    arrays["ka"] = asc(np.concatenate([k[:, :, 0:64], np.zeros((P, NDEC, 1), np.float32), k[:, :, 64:]], axis=2))
    arrays["va"] = asc(v["cache_a_v"][0].reshape(NDEC, 2, 64, P).transpose(2, 1, 0, 3))
    rows = PAST - rows_b_dist()
    k = v["cache_b_k"][0][:, rows].reshape(NDEC, KEYS_B, OT, P).transpose(2, 3, 0, 1)
    arrays["kb"] = asc(np.concatenate([k, np.zeros((OT, P, NDEC, 1), np.float32)], axis=3))
    vv = v["cache_b_v"][0][:, rows].reshape(NDEC, KEYS_B, OT, P)
    vv = np.concatenate([vv, np.zeros((NDEC, 384 - KEYS_B, OT, P), np.float32)], axis=1)
    arrays["vb"] = asc(vv.reshape(NDEC, 3, P, OT, P).transpose(3, 2, 1, 0, 4))
    outs = {
        "out_y": (P, MT, TOK), "out_ka": (P, TOK), "out_va": (P, TOK),
        "out_kb": (4, P, 2, TOK), "out_vb": (4, P, 2, TOK), "out_conv": (P, FT, 2 + 2 * NDEC),
    }
    nc = bacc.Bacc("TRN2", target_bir_lowering=False, num_devices=1)
    d = {n: nc.dram_tensor("in_" + n, a.shape, F32, kind="ExternalInput").ap() for n, a in arrays.items()}
    d.update({n: nc.dram_tensor(n, s, F32, kind="ExternalOutput").ap() for n, s in outs.items()})
    build(nc, d)
    r = run_bass_kernel_spmd(nc, [{"in_" + n: a for n, a in arrays.items()}], core_ids=[0]).results[0]

    y = r["out_y"].transpose(2, 1, 0).reshape(TOK, D_MODEL)
    ka, va = r["out_ka"].T.reshape(TOK, KV_A, HD), r["out_va"].T.reshape(TOK, KV_A, HD)
    kb, vb = (r[n].transpose(3, 0, 2, 1).reshape(TOK, H_B, HD) for n in ("out_kb", "out_vb"))
    cv = r["out_conv"].transpose(1, 0, 2).reshape(D_FF, 2 + 2 * NDEC)
    last = SEQ - WINDOW_A
    return (
        asc(y[None, :SEQ]), asc(y[SEQ:, None]),
        asc(ka[None, None, last:SEQ]), asc(va[None, None, last:SEQ]),
        asc(kb[None, None, :SEQ]), asc(vb[None, None, :SEQ]),
        asc(cv[:, 0:2].T[None, None]),
        asc(ka[None, SEQ:, None]), asc(va[None, SEQ:, None]),
        asc(kb[None, SEQ:, None]), asc(vb[None, SEQ:, None]),
        asc(cv[:, 2:].reshape(D_FF, NDEC, 2).transpose(1, 2, 0)[None]),
    )
```

```python
from contextlib import ExitStack

import numpy as np

import concourse.bass as bass
from concourse import mybir

F32 = mybir.dt.float32
F32R = mybir.dt.float32r
ALU = mybir.AluOpType
ACT = mybir.ActivationFunctionType
AX = mybir.AxisListType

P = 128
D_MODEL, D_FF = 2048, 5632
HD, H_A, KV_A, H_B = 64, 16, 2, 16
SEQ, NDEC, PAST = 256, 8, 2048
TOK = SEQ + NDEC
ROT, THETA, EPS = 16, 500000.0, 1e-6
SCALE = HD ** -0.5
WINDOW_A = 128
DILATIONS = ((128, 1), (512, 4), (2048, 16))
NEG = 1e30

MT = D_MODEL // P
OT = 8
FT = D_FF // P
CH = 1024
RING = 4
G_IN = 17
G_OUT = D_MODEL // 256
G_FF = D_FF // 256
N_IN, N_OUTA, N_OUTB, N_GU, N_DOWN = G_IN * 4, G_OUT * 2, G_OUT * 2, G_FF * 8, 2 * FT
CHUNKS = N_IN + N_OUTA + N_OUTB + N_GU + N_DOWN
SUMS = MT // 2
OWN = 2
AHEAD = 6
OUT_V = 5
STEPS = N_IN + N_OUTA
N_ATT = STEPS
B_OUTB = STEPS
B_GU = B_OUTB + N_OUTB
B_DOWN = B_GU + N_GU

KEYS_B = 320
KB = KEYS_B + 1
KA = WINDOW_A + 1
KSPLIT_B = ((0, 128), (128, 256), (256, KB))
KSPLIT_A = ((0, 65), (65, KA))

C_GPM, C_GQM, C_GPF, C_GQF = 0, 16, 32, 48
C_GOUT = 64
C_CW = 80
C_CB = C_CW + 3 * FT
C_ST = C_CB + FT
C_SINK = C_ST + FT * 16
C_SROW = C_SINK + H_A
N_PAR = C_SROW + 1
T_MA, T_MB, T_COS, T_SIN, T_MD = 0, 384, 768, 768 + TOK, 768 + 2 * TOK
N_TAB = T_MD + KB

SWAP = list(range(8, 16)) + list(range(0, 8)) + list(range(16, 32))


def groups_in():
    order = []
    for t in range(4):
        order += [("qB", t, 5 + t), ("kB", t, 9 + t), ("vB", t, 13 + t)]
    return order + [("kvA", 0, 4)] + [("qA", t, t) for t in range(4)]


GROUPS = groups_in()
GI = {(kind, t): gi for gi, (kind, t, _) in enumerate(GROUPS)}


def q_group(T):
    return GI[("qB", T)] if T < 4 else GI[("qA", T - 4)]


def group_end(gi):
    return 4 * (gi + 1) if gi < G_IN else N_IN + 2 * (gi - G_IN + 1)


STEP = {
    "T": [1, 1, 1, 1, 1, 1, 1, 1],
    "V": [2, 2, 2, 2, 2, 2, 2, 2],
    "qI": [-3, 2],
    "mul": [-2, 4],
    "bS": [2, 6],
    "bT": [3, 11],
    "pO": [3, 11],
    "pI": [3, 12],
    "bM": [7, 15],
    "bV": [8, 16],
    "gap": [3, 3, 3, 2],
    "s": [1, 2, 2, 1],
    "qk": [-3],
    "N0": [59],
    "W0": [60, 61, 62, 62, 64, 65, 66, 67],
    "ND0": [67],
    "aload": [63],
    "A": [57, 58, 59, 60, 61, 62, 63, 64, 65, 66, 67, 68, 69, 70, 71, 72],
    "aS": [70],
    "aT": [71],
    "aR": [74],
    "aV": [75],
    "N1": [76],
    "ND1": [77],
    "W1": [76, 77, 78, 79, 79, 80, 82, 82],
}


def make_plan():
    plan = {n: [] for n in range(-1, N_ATT + 1)}
    add = lambda n, *s: plan[n].append(s)
    for gi in range(G_IN):
        add(4 * gi + 4, "evac", gi)
    for g in range(G_OUT):
        add(N_IN + 2 * g + 2, "evac", G_IN + g)
    add(2, "ss")
    for t in range(4):
        e = 12 * t + 12
        gap = STEP["gap"][t]
        add(e + STEP["qk"][0], "qk", t)
        add(e + 1, "vtr", t)
        for a in range(4):
            s0 = e + STEP["s"][t] + gap * a
            add(s0, "S", t, a)
            add(s0 + STEP["T"][t], "T", t, a)
            add(s0 + STEP["V"][t], "V", t, a)
        add(s0 + STEP["V"][t], "O", t)
        for v in range(2):
            add(e + STEP["qI"][v], "qI", 2 * t + v)
            add(e + STEP["mul"][v], "mul", 2 * t + v)
            add(e + STEP["bS"][v], "bS", 2 * t + v)
            add(e + STEP["bT"][v], "bT", 2 * t + v)
            add(e + STEP["pO"][v], "pO", 2 * t + v)
            add(e + STEP["pI"][v], "pI", 2 * t + v)
            add(e + STEP["bM"][v], "bM", 2 * t + v)
            add(e + STEP["bV"][v], "bV", 2 * t + v)
    add(STEP["N0"][0], "N", 0)
    for j in range(OT):
        add(STEP["W0"][j], "W", 0, j)
    add(STEP["ND0"][0], "ND", 0)
    add(53, "vtr", 4)
    add(54, "vdec")
    add(STEP["aload"][0], "aload")
    for t in range(4):
        T = 4 + t
        for a in range(4):
            n = STEP["A"][4 * t + a]
            add(n, "S", T, a)
            add(n + STEP["T"][T], "T", T, a)
            add(n + STEP["V"][T], "V", T, a)
        add(n + 2, "L", T)
        add(n + STEP["V"][T] + 1, "O", T)
    for k in ("aS", "aT", "aR", "aV"):
        add(STEP[k][0], k)
    add(STEP["N1"][0], "N", 1)
    add(STEP["ND1"][0], "ND", 1)
    for j in range(OT):
        add(STEP["W1"][j], "W", 1, j)
    return plan


PLAN = make_plan()
ORDER = {}
for _n in sorted(PLAN):
    for _s in PLAN[_n]:
        ORDER.setdefault(_s[0], []).append(_s[1:])
MISC = [s for n in sorted(PLAN) for s in PLAN[n]
        if s[0] in ("ss", "qk", "vtr", "vdec", "aS", "aT", "aR", "aV", "W", "ND", "bT")]


def number(kind, *args):
    return ORDER[kind].index(args) + 1


def misc(kind, *args):
    return MISC.index((kind,) + args)


class Line:

    def __init__(self, eng, sem):
        self.eng, self.sem, self.n, self.at = eng, sem, 0, 0

    def do(self, ins):
        ins.then_inc(self.sem, 1)
        self.n += 1
        return self.n

    def need(self, n):
        self.eng.wait_ge(self.sem, self.at + n)

    def step(self, ins):
        self.need(self.do(ins))

    def loop(self, i, per):
        self.at, self.start, self.per = i * per, self.n, per

    def end(self, trips):
        assert self.n - self.start == self.per
        self.at = 0
        self.n = self.start + trips * self.per



def number_oh(kind, *args):
    return [s for n in sorted(PLAN) for s in PLAN[n] if s[0] in ("W", "ND")].index((kind,) + args) + 1


def build(nc, d, q_dram, p_dram):
    ctx = ExitStack()
    with ctx:
        def sem(name):
            return ctx.enter_context(nc.semaphore(name))

        def sb(name, shape, dt=F32, into=ctx):
            return into.enter_context(nc.sbuf_tensor(name, shape, dt))

        xT = sb("xT", [P, MT, TOK])
        raw = sb("raw", [P, RING, CH])
        wh = sb("wh", [P, RING, CH], F32R)
        wl = sb("wl", [P, RING, CH], F32R)
        par = sb("par", [P, N_PAR])
        ident = sb("ident", [P, P])
        ones = sb("ones", [P, P])
        eps = sb("eps", [P, 1])
        rB = sb("rB", [P, TOK])
        rms = sb("rms", [P, TOK])
        with ExitStack() as over:
            hh = sb("hh", [P, MT, TOK], F32R, over)
        ysq = sb("ysq", [P, MT, TOK])
        with ExitStack() as over:
            hl = sb("hl", [P, MT, TOK], F32R, over)
        yT = sb("yT", [P, MT, TOK])
        with ExitStack() as att:
            def sa(name, shape, dt=F32):
                return sb(name, shape, dt, att)
            tab = sa("tab", [P, N_TAB])
            oBh = sa("oBh", [P, OT, TOK], F32R)
            oBl = sa("oBl", [P, OT, TOK], F32R)
            qs = sa("qs", [P, 2, 2, TOK])
            ks = sa("ks", [P, 2, 2, TOK])
            vT = sa("vT", [P, 2, TOK])
            vn = sa("vn", [P, 2, 2, 256])
            vdec = sa("vdec", [NDEC, P])
            qk = sa("qk", [NDEC, 512])
            vself = sa("vself", [P, 4, 2, NDEC])
            qA = sa("qA", [P, NDEC, H_A])
            kA = sa("kA", [P, TOK])
            kdup = sa("kdup", [P, KV_A, TOK])
            vnA = sa("vnA", [P, 2, P])
            onat = sa("onat", [P, 2, OT * P])
            Sm = sa("Sm", [P, 2, 384])
            PT = sa("PT", [P, 2, 384])
            r1 = sa("r1", [P, 2, TOK])
            sh = sa("sh", [P, 2, TOK])
            junk = sh[:, :, 0:256]
            small = sa("small", [P, 128])
            od = sa("od", [P, 4, OT, NDEC])
            rd = sa("rd", [P, 3, NDEC])
            bSc = sa("bSc", [P, 48])
            bSm = sa("bSm", [16, KB])
            bP = sa("bP", [16, KB])
            with ExitStack() as a2:
                xsq = sb("xsq", [P, MT, TOK], F32, a2)
            with ExitStack() as a2:
                KtA = sb("KtA", [P, NDEC, KA], F32, a2)
                VtA = sb("VtA", [65, 2, NDEC, P], F32, a2)
                aSc = sb("aSc", [65, 256], F32, a2)
                aP = sb("aP", [P, KA], F32, a2)
                aPT = sb("aPT", [65, 256], F32, a2)
            with ExitStack() as a2:
                Kd = sb("Kd", [P, 3, NDEC, P], F32, a2)
                qb = sb("qb", [P, NDEC, P], F32, a2)
                Vd = sb("Vd", [P, NDEC, KB], F32, a2)
                Pb = sb("Pb", [P, NDEC, KB], F32, a2)
        NU = SEQ + 2 + 3 * NDEC
        with ExitStack() as ffn:
            gh = sb("gh", [P, FT, TOK], F32R, ffn)
            gl = sb("gl", [P, FT, TOK], F32R, ffn)
            U = sb("U", [P, 2, NU], F32, ffn)
            cv = sb("cv", [P, 2, NU - 2], F32, ffn)
            ge = sb("ge", [P, 2, TOK], F32, ffn)
            up = sb("up", [P, 2, TOK], F32, ffn)
            co = sb("co", [P, FT, 2 + 2 * NDEC], F32, ffn)
            sq, sqa = ge, up
            sq2 = cv[:, :, 0:TOK]
        U_dec = U[:, :, SEQ + 2:NU].rearrange("p k (s c) -> p k s c", c=3)

        def per_head(c):
            return small[:, c:c + 16].rearrange("p (t b a) -> p t b a", t=2, b=2)
        mn, ll, es, rl = (per_head(c) for c in (0, 16, 32, 48))
        ss4 = small[:, 64:68].rearrange("p (b c) -> p b c", b=2)
        ss2, rm2, ri2 = small[:, 68:70], small[:, 70:72], small[:, 72:74]
        amn, al, aes, ari = (small[:, c:c + 1] for c in (74, 75, 76, 77))
        bmn, bl, bri = (small[0:16, c:c + 1] for c in (78, 79, 80))
        sinkn = small[:, 82:82 + H_A + 1]

        ps = ctx.enter_context(nc.psum_tensor("ps", [P, 8, 512], F32))
        B_S, B_T, B_O, B_M = 4, 5, 6, 7

        x_landed = [sem(f"x_landed{c}") for c in range(4)]
        gains_landed, par_landed = sem("gains_landed"), sem("par_landed")
        tab_landed = sem("tab_landed")
        raw_landed = [sem(f"raw_landed{c}") for c in range(RING)]
        hi_ready = sem("hi_ready")
        lo_ready = sem("lo_ready")
        weights_used = sem("weights_used")
        xh_ready = sem("xh_ready")
        xl_ready = sem("xl_ready")
        const_ready = sem("const_ready")
        xsq_ready = sem("xsq_ready")
        evac_done = sem("evac_done")
        misc_ready = sem("misc_ready")
        misc_free = sem("misc_free")
        scores_ready = sem("scores_ready")
        masked_ready = sem("masked_ready")
        exp_ready = sem("exp_ready")
        pt_ready = sem("pt_ready")
        pt_copied = sem("pt_copied")
        pv_ready = sem("pv_ready")
        o_taken = sem("o_taken")
        sinkarg_ready = sem("sinkarg_ready")
        sinkexp_ready = sem("sinkexp_ready")
        kv_stored = [sem(f"kv_stored{c}") for c in range(2)]
        v_stored = sem("v_stored")
        KtA_landed, VtA_landed, VtA_full = sem("KtA_landed"), sem("VtA_landed"), sem("VtA_full")
        Kd_landed, Kd_full, Vd_landed = sem("Kd_landed"), sem("Kd_full"), sem("Vd_landed")
        q_out, qb_landed, p_out, Pb_landed = sem("q_out"), sem("qb_landed"), sem("p_out"), sem("Pb_landed")
        kq_ready = sem("kq_ready")
        bS_ready, bV_ready = sem("bS_ready"), sem("bV_ready")
        vp_ready = sem("vp_ready")
        norm_a = sem("norm_a")
        onat_scaled = sem("onat_scaled")
        oh_ready = sem("oh_ready")
        od_sq = sem("od_sq")
        od_sum = sem("od_sum")
        od_gained = sem("od_gained")
        aq_ready = sem("aq_ready")
        zero_ready = sem("zero_ready")
        a_min, a_exp, a_p = sem("a_min"), sem("a_exp"), sem("a_p")
        b_exp, b_p = sem("b_exp"), sem("b_p")
        ysq_ready, ysq_used = sem("ysq_ready"), sem("ysq_used")
        x1_ready, h2h_ready, h2l_ready = sem("x1_ready"), sem("h2h_ready"), sem("h2l_ready")
        sum_ready = sem("sum_ready")
        rB_ready = sem("rB_ready")
        state_ready, u_ready, tap_ready, conv_ready = (sem(n) for n in ("state_ready", "u_ready", "tap_ready", "conv_ready"))
        u_kept = sem("u_kept")
        gelu_ready, up_taken, g_ready, gh_ready, gl_ready = (
            sem(n) for n in ("gelu_ready", "up_taken", "g_ready", "gh_ready", "gl_ready"))
        down_done = sem("down_done")
        down_v = sem("down_v")
        out_ready = [sem(f"out_ready{c}") for c in range(MT // 2)]
        ysq2_ready = sem("ysq2_ready")
        yg_ready, yr_ready = sem("yg_ready"), sem("yr_ready")
        stored, other_stored = sem("stored"), sem("other_stored")
        dve_line, act_line, pool_line = sem("dve_line"), sem("act_line"), sem("pool_line")

        block = ctx.enter_context(nc.Block())

        def chunk(base, i, per, j):
            return i * per + (base + j), (base + j) % RING, i * (per // RING) + (base + j) // RING

        def heads_of(T, a):
            return slice(64 * (a % 2), 64 * (a % 2) + 64), a // 2

        @block.sync
        def _(sp):
            def load(c, src):
                n, slot, _ = c
                if not isinstance(n, int) or n >= RING:
                    sp.wait_ge(lo_ready, n - (RING - 1))
                sp.dma_start(raw[:, slot], src).then_inc(raw_landed[slot], 16)

            def stage(kind, *a):
                if kind == "ss":
                    sp.wait_ge(misc_ready, misc("ss") + 1)
                    sp.wait_ge(zero_ready, 1)
                    load_K(0)
                    load_V(0)
                elif kind == "bS" and a[0] + 1 < OT:
                    load_K(a[0] + 1)
                elif kind == "bM" and a[0] + 1 < OT:
                    load_V(a[0] + 1)
                elif kind == "qI":
                    u, = a
                    t, v = u // 2, u % 2
                    sp.wait_ge(misc_free, misc("qk", t) + 1)
                    sp.dma_start(Kd[64:65, 2], qk[:, 256 + P * v:256 + P * v + P]).then_inc(Kd_full, 16)
                    sp.wait_ge(q_out, 16 * (t + 1))
                    sp.dma_start(qb[:], q_dram[t, :, P * v:P * v + P].unsqueeze(0).to_broadcast([P, NDEC, P])
                                 ).then_inc(qb_landed, 16)
                elif kind == "pI":
                    u, = a
                    sp.wait_ge(p_out, 16 * (u + 1))
                    if u:
                        sp.wait_ge(bV_ready, u)
                    for h in range(2):
                        src = p_dram[u].rearrange("(s h) k -> h s k", h=2)[h].unsqueeze(0)
                        sp.dma_start(Pb[64 * h:64 * h + 64], src.to_broadcast([64, NDEC, KB])).then_inc(Pb_landed, 16)

            def load_K(u):
                if u:
                    sp.wait_ge(bS_ready, u)
                sp.dma_start(Kd[:, 0:2], d["kb"][u, :, 0:2]).then_inc(Kd_landed, 16)
                sp.dma_start(Kd[0:64, 2], d["kb"][u, 0:64, 2]).then_inc(Kd_landed, 16)

            def load_V(u):
                if u:
                    sp.wait_ge(vp_ready, u)
                sp.dma_start(Vd[:, :, 0:KEYS_B], d["vb"][u]).then_inc(Vd_landed, 16)

            sp.dma_start(par[:, 0:C_CW], d["par"][:, 0:C_CW]).then_inc(gains_landed, 16)
            sp.dma_start(xT[:, 0:4], d["x"][:, 0:4]).then_inc(x_landed[0], 16)
            load(chunk(0, 0, 4, 0), d["w_in"][GROUPS[0][2], 0])
            for c in range(1, 4):
                sp.dma_start(xT[:, 4 * c:4 * c + 4], d["x"][:, 4 * c:4 * c + 4]).then_inc(x_landed[c], 16)
                load(chunk(0, 0, 4, c), d["w_in"][GROUPS[0][2], c])
            sp.dma_start(par[:, C_CW:], d["par"][:, C_CW:]).then_inc(par_landed, 16)
            sp.dma_start(ident[:], d["ident"]).then_inc(tab_landed, 16)
            sp.dma_start(tab[:], d["tab"]).then_inc(tab_landed, 16)
            for n in range(4, N_IN):
                load(chunk(n, 0, 4, 0), d["w_in"][GROUPS[n // 4][2], n % 4])
                for s in PLAN.get(n - AHEAD, ()):
                    stage(*s)
            with sp.Fori(0, (N_OUTA + N_OUTB) // 4) as i:
                for j in range(4):
                    load(chunk(N_IN, i, 4, j), d["w_out"][i * 4 + j])
            with sp.Fori(0, G_FF) as i:
                for j in range(4):
                    load(chunk(B_GU, i, 8, j), d["w_gate"][i * 4 + j])
                for j in range(4):
                    load(chunk(B_GU, i, 8, 4 + j), d["w_up"][i * 4 + j])
            with sp.Fori(0, N_DOWN // 4) as i:
                for j in range(4):
                    load(chunk(B_DOWN, i, 4, j), d["w_down"][i * 4 + j])
            for jj in (0, 1, 5, 2, 3, 6, 4, 7):
                sp.wait_ge(out_ready[jj], 1)
                sp.dma_start(d["out_y"][:, 2 * jj:2 * jj + 2], yT[:, 2 * jj:2 * jj + 2]).then_inc(stored, 16)
            sp.wait_ge(stored, 16 * (MT // 2))

        @block.scalar
        def _(act):
            line = Line(act, act_line)

            def split(c):
                n, slot, lap = c
                act.wait_ge(raw_landed[slot], lap * 16 + 16)
                if not isinstance(n, int) or n >= RING:
                    act.wait_ge(weights_used, n - (RING - 1))
                nc.scalar.copy(wh[:, slot], raw[:, slot]).then_inc(hi_ready, 1)

            def free_misc(ins):
                ins.then_inc(misc_free, 1)

            def stage(kind, *a):
                if kind == "ss":
                    act.wait_ge(misc_ready, misc(kind, *a) + 1)
                    act.wait_ge(const_ready, 1)
                    free_misc(nc.scalar.activation(rms[:], ps[:, B_M, 0:TOK], ACT.Sqrt, bias=eps[:], scale=1.0 / D_MODEL))
                elif kind == "vtr":
                    T, = a
                    act.wait_ge(misc_ready, misc(kind, *a) + 1)
                    if 2 <= T < 4:
                        act.wait_ge(pv_ready, number("V", T - 2, 3))
                    if T == 4:
                        nc.scalar.copy(vnA[:], ps[:, B_M, 0:256].rearrange("p (b c) -> p b c", b=2)).then_inc(misc_free, 1)
                    else:
                        nc.scalar.copy(vn[:, T % 2], ps[:, B_M].rearrange("p (b c) -> p b c", b=2)).then_inc(misc_free, 1)
                elif kind == "vdec":
                    act.wait_ge(misc_ready, misc(kind) + 1)
                    nc.scalar.copy(vdec[:], ps[0:NDEC, B_M, 0:P]).then_inc(misc_free, 1)
                elif kind == "qk":
                    t, = a
                    act.wait_ge(misc_ready, misc(kind, *a) + 1)
                    if t:
                        act.wait_ge(q_out, 16 * t)
                        act.wait_ge(Kd_full, 16 * 2 * t)
                    nc.scalar.copy(qk[:], ps[0:NDEC, B_M]).then_inc(misc_free, 1)
                    act.wait_ge(misc_free, misc(kind, *a) + 1)
                    act.dma_start(q_dram[t], qk[:, 0:256]).then_inc(q_out, 16)
                elif kind == "S":
                    T, h = a
                    n = number(kind, *a)
                    p = n % 2
                    act.wait_ge(masked_ready, n)
                    line.do(nc.scalar.activation(Sm[:, p, 0:P], Sm[:, p, 0:P], ACT.Exp, scale=-1.0,
                                                 bias=mn[:, T % 2, 0, h:h + 1], accum_out=ll[:, T % 2, 0, h:h + 1]))
                    nc.scalar.activation(Sm[:, p, P:384], Sm[:, p, P:384], ACT.Exp, scale=-1.0,
                                         bias=mn[:, T % 2, 1, h:h + 1],
                                         accum_out=ll[:, T % 2, 1, h:h + 1]).then_inc(exp_ready, 1)
                elif kind == "T":
                    n = number(kind, *a)
                    act.wait_ge(pt_ready, n)
                    if n > 2:
                        act.wait_ge(pv_ready, n - 2)
                    nc.scalar.copy(PT[:, n % 2], ps[:, B_T, 0:384]).then_inc(pt_copied, 1)
                elif kind == "L":
                    T, = a
                    act.wait_ge(sinkarg_ready, T - 3)
                    nc.scalar.activation(es[:, T % 2], es[:, T % 2], ACT.Exp).then_inc(sinkexp_ready, 1)
                elif kind == "aS":
                    act.wait_ge(misc_ready, misc(kind, *a) + 1)
                    line.do(nc.scalar.copy(aSc[0:65, 0:128], ps[0:65, B_M, 0:128]))
                    nc.scalar.copy(aSc[0:64, 128:256], ps[0:64, B_M, 128:256]).then_inc(misc_free, 1)
                elif kind == "aT":
                    act.wait_ge(a_min, 1)
                    nc.scalar.activation(aP[:], ps[:, B_M, 0:KA], ACT.Exp, scale=-1.0, bias=amn,
                                         accum_out=al).then_inc(misc_free, 1)
                    nc.scalar.activation(aes, aes, ACT.Exp).then_inc(a_exp, 1)
                elif kind == "aR":
                    act.wait_ge(misc_ready, misc(kind, *a) + 1)
                    line.do(nc.scalar.copy(aPT[0:65, 0:128], ps[0:65, B_M, 0:128]))
                    nc.scalar.copy(aPT[0:64, 128:256], ps[0:64, B_M, 128:256]).then_inc(misc_free, 1)
                elif kind == "bT":
                    u, = a
                    act.wait_ge(misc_free, misc(kind, *a) + 1)
                    nc.scalar.activation(bP[:], bSm[:], ACT.Exp, scale=-1.0, bias=bmn, accum_out=bl).then_inc(b_exp, 1)
                elif kind == "pO":
                    u, = a
                    act.wait_ge(b_p, u + 1)
                    act.dma_start(p_dram[u], bP[:]).then_inc(p_out, 16)
                elif kind == "bV":
                    u, = a
                    act.wait_ge(vp_ready, u + 1)
                    for s in range(NDEC):
                        ins = nc.scalar.activation(Pb[:, s], Pb[:, s], ACT.Identity, accum_out=od[:, 0, u, s:s + 1])
                        if s < NDEC - 1:
                            line.do(ins)
                    ins.then_inc(bV_ready, 1)
                elif kind == "N":
                    X, = a
                    act.wait_ge(o_taken, 4 * X + 4)
                    for b in range(2):
                        for c in range(2):
                            k = line.do(nc.scalar.activation(
                                junk, onat[:, b, 512 * c:512 * c + 512].rearrange("p (x y) -> p x y", x=2),
                                ACT.Square, accum_out=ss4[:, b, c:c + 1]))
                            line.need(k)
                    for b in range(2):
                        k = line.do(nc.scalar.activation(ss2[:, b:b + 1], ss4[:, b, 1:2], ACT.Identity, bias=ss4[:, b, 0:1]))
                    line.need(k)
                    nc.scalar.activation(rm2, ss2, ACT.Sqrt, bias=eps[:], scale=1.0 / (OT * P)).then_inc(norm_a, 1)
                elif kind == "W":
                    X, j = a
                    act.wait_ge(misc_ready, misc(kind, *a) + 1)
                    dst = oBh[:, j, 0:SEQ] if X == 0 else hh[:, j, 0:SEQ]
                    nc.scalar.activation(dst, ps[:, B_M, 0:SEQ], ACT.Copy,
                                         scale=par[:, C_GOUT + 8 * X + j:C_GOUT + 8 * X + j + 1]).then_inc(oh_ready, 1)
                elif kind == "ND":
                    X, = a
                    act.wait_ge(od_sum, X + 1)
                    nc.scalar.activation(rd[:, 1], rd[:, 0], ACT.Sqrt, bias=eps[:], scale=1.0 / (OT * P)).then_inc(norm_a, 1)
                    act.wait_ge(od_gained, X + 1)
                    dst = oBh[:, :, SEQ:TOK] if X == 0 else hh[:, 0:OT, SEQ:TOK]
                    nc.scalar.copy(dst, od[:, 3]).then_inc(oh_ready, 1)

            act.wait_ge(const_ready, 1)
            line.do(nc.scalar.activation(small[:, 100:101], eps[:], ACT.Copy))
            act.wait_ge(gains_landed, 16)
            for j in range(MT):
                if j % 4 == 0:
                    act.wait_ge(x_landed[j // 4], 16)
                nc.scalar.activation(hh[:, j], xT[:, j], ACT.Copy,
                                     scale=par[:, C_GPM + j:C_GPM + j + 1]).then_inc(xh_ready, 1)
                if j in (3, 7, 11):
                    split(chunk(0, 0, 4, j // 4))
            for n in range(N_ATT):
                split(chunk(0, 0, 4, n + 3))
                for s in PLAN[n]:
                    stage(*s)
            for s in PLAN[N_ATT]:
                stage(*s)

            act.wait_ge(const_ready, 1)
            line.step(nc.scalar.activation(small[:, 100:101], eps[:], ACT.Sqrt))
            with act.Fori(0, G_OUT // 2) as i:
                line.loop(i, 2)
                for g in range(2):
                    for j in range(2):
                        split(chunk(B_OUTB, i, 4, 2 * g + j + 3))
                    act.wait_ge(evac_done, i * 2 + (G_IN + G_OUT + g + 1))
                    act.wait_ge(ysq_used, i * 2 + (g + 1))
                    nc.scalar.activation(sq[:], yT[:, bass.ds(i * 4 + 2 * g, 2)], ACT.Square).then_inc(ysq_ready, 1)
                    act.wait_ge(ysq_ready, i * 2 + (g + 1))
                    for k in range(2):
                        y1 = yT[:, bass.ds(i * 4 + (2 * g + k), 1)]
                        ins = nc.scalar.activation(y1, y1, ACT.Copy, scale=par[:, bass.ds(i * 4 + (C_GQM + 2 * g + k), 1)])
                        if k == 0:
                            line.do(ins)
                        else:
                            ins.then_inc(yg_ready, 1)
            line.end(G_OUT // 2)
            act.wait_ge(sum_ready, 1)
            nc.scalar.activation(rms[:], ps[:, B_M, 0:TOK], ACT.Sqrt, bias=eps[:], scale=1.0 / D_MODEL).then_inc(norm_a, 1)
            for jj in range(MT // 2):
                act.wait_ge(x1_ready, jj + 1)
                for j in (2 * jj, 2 * jj + 1):
                    nc.scalar.activation(hh[:, j], xT[:, j], ACT.Copy,
                                         scale=par[:, C_GPF + j:C_GPF + j + 1]).then_inc(h2h_ready, 1)

            def ffn_gate(i, first):
                early = 6 if first else 4
                for j in range(early):
                    split(chunk(B_GU, i, 8, j + 3))
                    if first and j < 4:
                        for jj in (2 * j, 2 * j + 1):
                            if jj >= 2:
                                act.wait_ge(ysq_used, SUMS + jj)
                            nc.scalar.activation(sq2 if jj % 2 else sq[:], xT[:, 2 * jj:2 * jj + 2], ACT.Square).then_inc(ysq_ready, 1)
                if first:
                    act.wait_ge(sum_ready, 2)
                    nc.scalar.activation(rms[:], ps[:, B_M, 0:TOK], ACT.Sqrt, bias=eps[:],
                                         scale=1.0 / D_MODEL).then_inc(norm_a, 1)
                act.wait_ge(u_ready, i + 1)
                for k in range(2):
                    nc.scalar.activation(cv[:, k], U[:, k, 0:NU - 2], ACT.Identity,
                                         scale=par[:, bass.ds(i * 2 + (C_CW + k), 1)],
                                         bias=par[:, bass.ds(i * 2 + (C_CB + k), 1)]).then_inc(tap_ready, 1)
                if not first:
                    split(chunk(B_GU, i, 8, 7))
                act.wait_ge(conv_ready, i + 1)
                line.do(nc.scalar.activation(ge[:, :, 0:SEQ], cv[:, :, 0:SEQ], ACT.Gelu_apprx_tanh))
                nc.scalar.activation(ge[:, :, SEQ:TOK], cv[:, :, SEQ + 2:NU - 2:3], ACT.Gelu_apprx_tanh).then_inc(gelu_ready, 1)
                for j in range(max(5, early), 8):
                    split(chunk(B_GU, i, 8, j + 3))
                act.wait_ge(g_ready, i + 1)
                nc.scalar.copy(gh[:, bass.ds(i * 2, 2)], up[:]).then_inc(gh_ready, 1)

            ffn_gate(0, True)
            line.loop(0, 1)
            with act.Fori(0, G_FF - 1) as i:
                line.loop(i, 1)
                ffn_gate(i + 1, False)
            line.end(G_FF - 1)

            line.step(nc.scalar.activation(sq[:, 0, 0:1], eps[:], ACT.Sqrt))
            for half in range(2):
                with act.Fori(0, FT // 4 - half) as i:
                    for j in range(4):
                        split(chunk(B_DOWN + FT * half, i, 4, j + 3))
                if half == 1:
                    split(chunk(B_DOWN + FT, FT // 4 - 1, 4, 3))
                for m in range(8):
                    if m < 7:
                        act.wait_ge(down_done, 7 * half + m + 1)
                    else:
                        act.wait_ge(weights_used, B_DOWN + FT * (half + 1))
                    nc.scalar.activation(ysq[:, 8 * half + m], ps[:, (m + 4) % 8, 0:TOK], ACT.Square).then_inc(ysq2_ready, 1)
            act.wait_ge(sum_ready, 3)
            nc.scalar.activation(rms[:], ps[:, 4, 0:TOK], ACT.Sqrt, bias=eps[:], scale=1.0 / D_MODEL).then_inc(norm_a, 1)

        @block.vector
        def _(dve):
            line = Line(dve, dve_line)
            V = nc.vector

            def split(c):
                n, slot, _ = c
                dve.wait_ge(hi_ready, n + 1)
                V.tensor_tensor(wl[:, slot], raw[:, slot], wh[:, slot].bitcast(F32), ALU.subtract).then_inc(lo_ready, 1)

            def wide(x, n=2):
                return x.unsqueeze(1).to_broadcast([x.shape[0], n, x.shape[1]])

            def rotate(dst, src, n, scale, signal=None):
                cos, sin = wide(tab[:, T_COS:T_COS + TOK], n), wide(tab[:, T_SIN:T_SIN + TOK], n)
                line.do(V.scalar_tensor_tensor(r1[:, 0:n], src, scale, cos, ALU.mult, ALU.mult))
                line.step(V.stream_shuffle(sh[:, 0:n], src, SWAP))
                line.step(V.scalar_tensor_tensor(sh[:, 0:n], sh[:, 0:n], scale, sin, ALU.mult, ALU.mult))
                return V.tensor_tensor(dst, r1[:, 0:n], sh[:, 0:n], ALU.add)

            def evac(gi):
                dve.wait_ge(weights_used, group_end(gi))
                b = 2 * (gi % 2)
                src = ps[:, b:b + 2, 0:TOK]
                if gi >= G_IN:
                    g = gi - G_IN
                    V.tensor_copy(yT[:, 2 * g:2 * g + 2], src).then_inc(evac_done, 1)
                    return
                kind, t, _ = GROUPS[gi]
                if kind == "kvA":
                    line.step(rotate(kA[:].unsqueeze(1), src[:, 0:1], 1, 1.0))
                    dve.wait_ge(v_stored, 16 * 4)
                    dve.wait_ge(misc_ready, misc("vtr", 3) + 1)
                    line.do(V.tensor_tensor(vT[:, 0], src[:, 1], rB[:], ALU.mult))
                    line.do(V.tensor_copy(kdup[0:64, 0], kA[0:64]))
                    line.do(V.tensor_copy(kdup[64:128, 0], kA[0:64]))
                    line.do(V.tensor_copy(kdup[0:64, 1], kA[64:128]))
                    V.tensor_copy(kdup[64:128, 1], kA[64:128]).then_inc(evac_done, 1)
                elif kind == "qB":
                    if t >= 2:
                        dve.wait_ge(scores_ready, number("S", t - 2, 3))
                        dve.wait_ge(misc_ready, misc("qk", t - 2) + 1)
                    rotate(qs[:, t % 2], src, 2, -SCALE).then_inc(evac_done, 1)
                elif kind == "qA":
                    dve.wait_ge(scores_ready, number("S", t + 2, 3))
                    line.step(rotate(qs[:, t % 2], src, 2, -SCALE))
                    kv = t // 2
                    for half in range(2):
                        h0 = 8 * kv + 4 * (t % 2) + half
                        ins = V.tensor_copy(
                            qA[64 * kv:64 * kv + 64, :, h0:h0 + 3:2].rearrange("p s i -> p i s"),
                            qs[64 * half:64 * half + 64, t % 2, :, SEQ:TOK])
                        if half == 0:
                            line.do(ins)
                        else:
                            ins.then_inc(evac_done, 1)
                elif kind == "kB":
                    if t >= 2:
                        dve.wait_ge(scores_ready, number("S", t - 2, 3))
                        dve.wait_ge(misc_ready, misc("qk", t - 2) + 1)
                        dve.wait_ge(kv_stored[t % 2], 16)
                    rotate(ks[:, t % 2], src, 2, 1.0).then_inc(evac_done, 1)
                else:
                    if t:
                        dve.wait_ge(v_stored, 16 * t)
                        dve.wait_ge(misc_ready, misc("vtr", t - 1) + 1)
                    line.step(V.tensor_tensor(vT[:], src, wide(rB[:]), ALU.mult))
                    V.tensor_copy(vself[:, t], vT[:, :, SEQ:TOK]).then_inc(evac_done, 1)

            def stage(kind, *a):
                if kind == "evac":
                    evac(*a)
                elif kind == "ss":
                    dve.wait_ge(misc_free, misc(kind, *a) + 1)
                    dve.wait_ge(misc_ready, misc(kind, *a) + 1)
                    dve.wait_ge(tab_landed, 32)
                    dve.wait_ge(par_landed, 16)
                    line.do(V.tensor_scalar(sinkn, par[:, C_SINK:C_SINK + H_A + 1], -1.0, None, ALU.mult))
                    line.step(V.reciprocal(rB[:], rms[:]))
                    line.do(V.tensor_tensor(tab[:, T_COS:T_COS + TOK], tab[:, T_COS:T_COS + TOK], rB[:], ALU.mult))
                    line.do(V.tensor_tensor(tab[:, T_SIN:T_SIN + TOK], tab[:, T_SIN:T_SIN + TOK], rB[:], ALU.mult))
                    line.step(V.memset(qA[:], 0.0))
                    V.memset(Kd[64:128, 2], 0.0).then_inc(zero_ready, 1)
                elif kind == "S":
                    T, h = a
                    n = number(kind, *a)
                    p = n % 2
                    dve.wait_ge(scores_ready, n)
                    if n > 2:
                        dve.wait_ge(pt_ready, n - 2)
                    if h == 0 and T >= 2:
                        dve.wait_ge(exp_ready, number("S", T - 2, 3))
                    m = T_MB if T < 4 else T_MA
                    init = NEG if T < 4 else sinkn[:, 4 * (T - 4) + h:4 * (T - 4) + h + 1]
                    line.do(V.tensor_tensor_reduce(
                        out=Sm[:, p, 0:P], in0=ps[:, B_S, 0:P], in1=tab[:, m:m + P], scale=1.0, scalar=init,
                        op0=ALU.add, op1=ALU.min, accum_out=mn[:, T % 2, 0, h:h + 1]))
                    V.tensor_tensor_reduce(
                        out=Sm[:, p, P:384], in0=ps[:, B_S, P:384], in1=tab[:, m + P:m + 384], scale=1.0, scalar=init,
                        op0=ALU.add, op1=ALU.min, accum_out=mn[:, T % 2, 1, h:h + 1]).then_inc(masked_ready, 1)
                elif kind == "L":
                    T, = a
                    dve.wait_ge(masked_ready, number("S", T, 3))
                    sk = par[:, C_SINK + 4 * (T - 4):C_SINK + 4 * (T - 4) + 4]
                    V.tensor_tensor(es[:, T % 2], mn[:, T % 2], wide(sk), ALU.add).then_inc(sinkarg_ready, 1)
                elif kind == "O":
                    T, = a
                    dve.wait_ge(pv_ready, number("V", T, 3))
                    dve.wait_ge(exp_ready, number("S", T, 3))
                    if T >= 4:
                        dve.wait_ge(misc_ready, misc("W", 0, 2 * (T - 4) + 1) + 1)
                    if T >= 4:
                        dve.wait_ge(sinkexp_ready, T - 3)
                        line.step(V.tensor_tensor(ll[:, T % 2], ll[:, T % 2], es[:, T % 2], ALU.add))
                    line.step(V.reciprocal(rl[:, T % 2], ll[:, T % 2]))
                    c = 256 * (T % 4)
                    for b in range(2):
                        ins = V.tensor_tensor(
                            onat[:, b, c:c + 256].rearrange("p (a e) -> p a e", a=4),
                            ps[:, B_O, 256 * b:256 * b + 256].rearrange("p (a e) -> p a e", a=4),
                            rl[:, T % 2, b].unsqueeze(2).to_broadcast([P, 4, HD]), ALU.mult)
                        if b == 0:
                            line.do(ins)
                        else:
                            ins.then_inc(o_taken, 1)
                elif kind == "aT":
                    dve.wait_ge(misc_ready, misc(kind, *a) + 1)
                    line.step(V.tensor_reduce(amn, ps[:, B_M, 0:KA], AX.X, ALU.min))
                    line.step(V.tensor_tensor(amn, amn, sinkn[:, H_A:H_A + 1], ALU.min))
                    V.tensor_tensor(aes, amn, par[:, C_SROW:C_SROW + 1], ALU.add).then_inc(a_min, 1)
                    dve.wait_ge(a_exp, 1)
                    line.step(V.tensor_tensor(al, al, aes, ALU.add))
                    line.step(V.reciprocal(ari, al))
                    V.tensor_scalar(aP[:], aP[:], ari, None, ALU.mult).then_inc(a_p, 1)
                elif kind == "aV":
                    dve.wait_ge(misc_ready, misc(kind, *a) + 1)
                    o = ps[:, B_M, 0:P].rearrange("p (s h) -> p s h", h=H_A)
                    for kv in range(2):
                        for half in range(2):
                            ins = V.tensor_copy(
                                od[64 * half:64 * half + 64, 0, 4 * kv:4 * kv + 4, :].rearrange("p i s -> p s i"),
                                o[64 * kv:64 * kv + 64, :, 8 * kv + half:8 * kv + 8:2])
                            if (kv, half) == (1, 1):
                                ins.then_inc(misc_free, 1)
                            else:
                                line.do(ins)
                elif kind == "bS":
                    u, = a
                    dve.wait_ge(kq_ready, u + 1)
                    if u:
                        dve.wait_ge(misc_ready, misc("bT", u - 1) + 1)
                    V.tensor_reduce(bSc[:], Kd[:].rearrange("p c s (h e) -> p (c s h) e", h=2), AX.X,
                                    ALU.add).then_inc(bS_ready, 1)
                elif kind == "bT":
                    u, = a
                    dve.wait_ge(misc_ready, misc(kind, *a) + 1)
                    if u:
                        dve.wait_ge(p_out, 16 * u)
                    V.tensor_tensor_reduce(
                        out=bSm[:], in0=ps[0:16, B_M, 0:KB], in1=tab[0:16, T_MD:T_MD + KB], scale=1.0, scalar=NEG,
                        op0=ALU.add, op1=ALU.min, accum_out=bmn).then_inc(misc_free, 1)
                    dve.wait_ge(b_exp, u + 1)
                    line.step(V.reciprocal(bri, bl))
                    V.tensor_scalar(bP[:], bP[:], bri, None, ALU.mult).then_inc(b_p, 1)
                elif kind == "N":
                    X, = a
                    dve.wait_ge(norm_a, 2 * X + 1)
                    line.step(V.reciprocal(ri2, rm2))
                    for b in range(2):
                        ins = V.tensor_scalar(onat[:, b], onat[:, b], ri2[:, b:b + 1], None, ALU.mult)
                        if b == 0:
                            line.do(ins)
                        else:
                            ins.then_inc(onat_scaled, 1)
                elif kind == "W":
                    X, j = a
                    dve.wait_ge(oh_ready, number_oh(kind, *a))
                    hi = oBh[:, j, 0:SEQ] if X == 0 else hh[:, j, 0:SEQ]
                    lo = oBl[:, j, 0:SEQ] if X == 0 else hh[:, OT + j, 0:SEQ]
                    V.scalar_tensor_tensor(lo, ps[:, B_M, 0:SEQ], par[:, C_GOUT + 8 * X + j:C_GOUT + 8 * X + j + 1],
                                           hi.bitcast(F32), ALU.mult, ALU.subtract).then_inc(misc_free, 1)
                elif kind == "ND":
                    X, = a
                    if X == 0:
                        dve.wait_ge(bV_ready, OT)
                    else:
                        dve.wait_ge(misc_free, misc("aV") + 1)
                    V.tensor_tensor(od[:, 1], od[:, 0], od[:, 0], ALU.mult).then_inc(od_sq, 1)
                    dve.wait_ge(misc_ready, misc(kind, *a) + 1)
                    V.tensor_reduce(rd[:, 0], ps[:, B_M, 0:OT * NDEC].rearrange("p (j s) -> p s j", s=NDEC),
                                    AX.X, ALU.add).then_inc(od_sum, 1)
                    dve.wait_ge(norm_a, 2 * X + 2)
                    line.step(V.reciprocal(rd[:, 2], rd[:, 1]))
                    line.step(V.tensor_tensor(od[:, 2], od[:, 0], wide(rd[:, 2], OT), ALU.mult))
                    g = par[:, C_GOUT + 8 * X:C_GOUT + 8 * X + 8].unsqueeze(2).to_broadcast([P, OT, NDEC])
                    V.tensor_tensor(od[:, 3], od[:, 2], g, ALU.mult).then_inc(od_gained, 1)
                    dve.wait_ge(oh_ready, number_oh(kind, *a))
                    dve.wait_ge(od_gained, X + 1)
                    hi = oBh[:, :, SEQ:TOK] if X == 0 else hh[:, 0:OT, SEQ:TOK]
                    lo = oBl[:, :, SEQ:TOK] if X == 0 else hh[:, OT:2 * OT, SEQ:TOK]
                    V.tensor_tensor(lo, od[:, 3], hi.bitcast(F32), ALU.subtract).then_inc(misc_free, 1)

            V.memset(eps[:], EPS).then_inc(const_ready, 1)
            V.memset(ones[:], 1.0).then_inc(const_ready, 1)
            dve.wait_ge(gains_landed, 16)
            for j in range(MT):
                dve.wait_ge(xh_ready, j + 1)
                V.scalar_tensor_tensor(hl[:, j], xT[:, j], par[:, C_GPM + j:C_GPM + j + 1],
                                       hh[:, j].bitcast(F32), ALU.mult, ALU.subtract).then_inc(xl_ready, 1)
                if j in (3, 7):
                    split(chunk(0, 0, 4, j // 4))
            for n in range(N_ATT):
                split(chunk(0, 0, 4, n + 2))
                for s in PLAN[n]:
                    stage(*s)
            for s in PLAN[N_ATT]:
                stage(*s)

            with dve.Fori(0, G_OUT // 2) as i:
                for g in range(2):
                    for j in range(2):
                        split(chunk(B_OUTB, i, 4, 2 * g + j + 2))
                    dve.wait_ge(weights_used, i * 4 + (B_OUTB + 2 * g + 2))
                    b = 2 * ((G_IN + G_OUT + g) % 2)
                    y2 = yT[:, bass.ds(i * 4 + 2 * g, 2)]
                    V.tensor_tensor(y2, ps[:, b:b + 2, 0:TOK], y2, ALU.add).then_inc(evac_done, 1)
            dve.wait_ge(norm_a, 5)
            V.reciprocal(rB[:], rms[:]).then_inc(rB_ready, 1)
            dve.wait_ge(rB_ready, 1)

            def low(jj):
                for j in (2 * jj, 2 * jj + 1):
                    dve.wait_ge(h2h_ready, j + 1)
                    V.scalar_tensor_tensor(hl[:, j], xT[:, j], par[:, C_GPF + j:C_GPF + j + 1],
                                           hh[:, j].bitcast(F32), ALU.mult, ALU.subtract).then_inc(h2l_ready, 1)

            for jj in range(MT // 2):
                y2, x2 = yT[:, 2 * jj:2 * jj + 2], xT[:, 2 * jj:2 * jj + 2]
                if jj < OWN:
                    dve.wait_ge(yg_ready, G_OUT)
                    line.step(V.tensor_tensor(y2, y2, wide(rB[:]), ALU.mult))
                else:
                    dve.wait_ge(yr_ready, jj - OWN + 1)
                V.tensor_tensor(x2, x2, y2, ALU.add).then_inc(x1_ready, 1)
                if jj:
                    low(jj - 1)
            low(MT // 2 - 1)

            def ffn(i, first):
                early = 6 if first else 4
                for j in range(early):
                    split(chunk(B_GU, i, 8, j + 2))
                if first:
                    dve.wait_ge(norm_a, 6)
                    V.reciprocal(rB[:], rms[:]).then_inc(rB_ready, 1)
                    dve.wait_ge(rB_ready, 2)
                dve.wait_ge(weights_used, i * 8 + (B_GU + 4))
                dve.wait_ge(state_ready, i + 1)
                line.do(V.tensor_tensor(U[:, :, 2:2 + SEQ], ps[:, 0:2, 0:SEQ], wide(rB[:, 0:SEQ]), ALU.mult))
                V.tensor_tensor(U_dec[:, :, :, 2], ps[:, 0:2, SEQ:TOK], wide(rB[:, SEQ:TOK]), ALU.mult).then_inc(u_ready, 1)
                if not first:
                    split(chunk(B_GU, i, 8, 6))
                dve.wait_ge(tap_ready, i * 2 + 2)
                for tap in (1, 2):
                    for k in range(2):
                        ins = V.scalar_tensor_tensor(
                            cv[:, k], U[:, k, tap:tap + NU - 2],
                            par[:, bass.ds(i * 2 + (C_CW + FT * tap + k), 1)], cv[:, k], ALU.mult, ALU.add)
                        if (tap, k) == (2, 1):
                            ins.then_inc(conv_ready, 1)
                        else:
                            n = line.do(ins)
                    if tap == 1:
                        line.need(n)
                for j in range(max(5, early), 8):
                    split(chunk(B_GU, i, 8, j + 2))
                dve.wait_ge(weights_used, i * 8 + (B_GU + 8))
                V.tensor_tensor(up[:], ps[:, 2:4, 0:TOK], wide(rB[:]), ALU.mult).then_inc(up_taken, 1)
                dve.wait_ge(up_taken, i + 1)
                dve.wait_ge(gelu_ready, i + 1)
                V.tensor_tensor(up[:], up[:], ge[:], ALU.mult).then_inc(g_ready, 1)
                dve.wait_ge(g_ready, i + 1)
                dve.wait_ge(gh_ready, i + 1)
                V.tensor_tensor(gl[:, bass.ds(i * 2, 2)], up[:], gh[:, bass.ds(i * 2, 2)].bitcast(F32),
                                ALU.subtract).then_inc(gl_ready, 1)

            ffn(0, True)
            with dve.Fori(0, G_FF - 1) as i:
                line.loop(i, 4)
                ffn(i + 1, False)
            line.end(G_FF - 1)

            for half in range(2):
                with dve.Fori(0, FT // 4 - half) as i:
                    for j in range(4):
                        split(chunk(B_DOWN + FT * half, i, 4, j + 2))
                if half == 1:
                    for j in range(2):
                        split(chunk(B_DOWN + FT, FT // 4 - 1, 4, j + 2))
                for m in range(8):
                    dve.wait_ge(ysq2_ready, 8 * half + m + 1)
                    j = 8 * half + m
                    V.tensor_scalar(yT[:, j], ps[:, (m + 4) % 8, 0:TOK], par[:, C_GQF + j:C_GQF + j + 1], None,
                                    ALU.mult).then_inc(down_v, 1)
            dve.wait_ge(norm_a, 7)
            V.reciprocal(rB[:], rms[:]).then_inc(rB_ready, 1)
            dve.wait_ge(rB_ready, 3)
            dve.wait_ge(down_v, MT)
            for jj in range(OUT_V):
                y2, x2 = yT[:, 2 * jj:2 * jj + 2], xT[:, 2 * jj:2 * jj + 2]
                line.step(V.tensor_tensor(y2, y2, wide(rB[:]), ALU.mult))
                V.tensor_tensor(y2, y2, x2, ALU.add).then_inc(out_ready[jj], 1)

        @block.gpsimd
        def _(pool):
            line = Line(pool, pool_line)
            G = nc.gpsimd

            def stage(kind, *a):
                if kind == "evac":
                    gi, = a
                    if gi >= G_IN:
                        return
                    what, t, _ = GROUPS[gi]
                    if what == "kvA":
                        pool.wait_ge(evac_done, gi + 1)
                        G.dma_start(d["out_ka"], kA[:]).then_inc(other_stored, 16)
                        G.dma_start(d["out_va"], vT[:, 0]).then_inc(v_stored, 16)
                    elif what == "kB":
                        pool.wait_ge(evac_done, gi + 1)
                        G.dma_start(d["out_kb"][t], ks[:, t % 2]).then_inc(kv_stored[t % 2], 16)
                    elif what == "vB":
                        pool.wait_ge(evac_done, gi + 1)
                        G.dma_start(d["out_vb"][t], vT[:]).then_inc(v_stored, 16)
                elif kind == "mul":
                    u, = a
                    pool.wait_ge(Kd_landed, 32 * (u + 1))
                    pool.wait_ge(Kd_full, 16 * (u + 1))
                    pool.wait_ge(qb_landed, 16 * (u + 1))
                    G.tensor_tensor(Kd[:], Kd[:], qb[:].unsqueeze(1).to_broadcast([P, 3, NDEC, P]),
                                    ALU.mult).then_inc(kq_ready, 1)
                elif kind == "bM":
                    u, = a
                    pool.wait_ge(Vd_landed, 16 * (u + 1))
                    pool.wait_ge(evac_done, GI[("vB", u // 2)] + 1)
                    line.step(G.tensor_copy(Vd[:, :, KEYS_B], vself[:, u // 2, u % 2]))
                    pool.wait_ge(Pb_landed, 32 * (u + 1))
                    G.tensor_tensor(Pb[:], Pb[:], Vd[:], ALU.mult).then_inc(vp_ready, 1)
                elif kind == "aload":
                    pool.wait_ge(bV_ready, OT)
                    G.dma_start(KtA[:], d["ka"]).then_inc(KtA_landed, 16)
                    G.dma_start(VtA[0:64], d["va"]).then_inc(VtA_landed, 16)
                    pool.wait_ge(KtA_landed, 16)
                    G.tensor_copy(KtA[:, :, 64], kA[:, SEQ:TOK]).then_inc(aq_ready, 1)
                    pool.wait_ge(VtA_landed, 16)
                    pool.wait_ge(misc_free, misc("vdec") + 1)
                    G.dma_start(VtA[64:65, 0], vdec[:]).then_inc(VtA_full, 16)

            for c in range(4):
                pool.wait_ge(x_landed[c], 16)
                G.tensor_tensor(xsq[:, 4 * c:4 * c + 4], xT[:, 4 * c:4 * c + 4], xT[:, 4 * c:4 * c + 4],
                                ALU.mult).then_inc(xsq_ready, 1)
            for n in range(N_ATT + 1):
                for s in PLAN[n]:
                    stage(*s)

            def clear_squares():
                G.memset(sqa[:], 0.0).then_inc(ysq_used, 1)

            def add_squares(c, k):
                pool.wait_ge(ysq_ready, k + (8 * c + 1))
                pool.wait_ge(ysq_used, k + (SUMS * c + 1))
                src = sq2 if c == 1 and k % 2 else sq[:]
                G.tensor_tensor(sqa[:], sqa[:], src, ALU.add).then_inc(ysq_used, 1)

            pool.wait_ge(misc_free, len(MISC))
            clear_squares()
            with pool.Fori(0, G_OUT - 1) as i:
                add_squares(0, i)
            pool.wait_ge(sum_ready, 1)
            clear_squares()
            pool.wait_ge(rB_ready, 1)
            pool.wait_ge(yg_ready, G_OUT)
            for jj in range(OWN, MT // 2):
                y2 = yT[:, 2 * jj:2 * jj + 2]
                G.tensor_tensor(y2, y2, rB[:].unsqueeze(1).to_broadcast([P, 2, TOK]), ALU.mult).then_inc(yr_ready, 1)
            for jj in range(MT // 2 - 1):
                add_squares(1, jj)
            pool.wait_ge(sum_ready, 2)
            line.step(G.memset(U[:], 0.0))

            def window(i):
                if not isinstance(i, int) or i > 0:
                    pool.wait_ge(conv_ready, i)
                    pool.wait_ge(u_kept, i)
                G.tensor_copy(U_dec[:, :, :, 0:2],
                              par[:, bass.ds(i * (32) + C_ST, 32)].rearrange("p (k s c) -> p k s c", k=2, c=2)
                              ).then_inc(state_ready, 1)
                pool.wait_ge(u_ready, i + 1)
                line.do(G.tensor_copy(co[:, bass.ds(i * 2, 2), 0:2], U[:, :, SEQ:SEQ + 2]))
                G.tensor_copy(co[:, bass.ds(i * 2, 2), 2:2 + 2 * NDEC].rearrange("p k (s c) -> p k s c", c=2),
                              U_dec[:, :, :, 1:3]).then_inc(u_kept, 1)

            window(0)
            with pool.Fori(0, G_FF - 1) as i:
                line.loop(i, 1)
                window(i + 1)
            line.end(G_FF - 1)
            pool.wait_ge(u_kept, G_FF)
            G.dma_start(d["out_conv"], co[:]).then_inc(other_stored, 16)
            pool.wait_ge(gl_ready, G_FF)
            clear_squares()
            for k in range(MT // 2 - 3):
                pool.wait_ge(ysq2_ready, 2 * k + 2)
                pool.wait_ge(ysq_used, 2 * SUMS + 1 + k)
                G.tensor_tensor(sqa[:], sqa[:], ysq[:, 2 * k:2 * k + 2], ALU.add).then_inc(ysq_used, 1)
            pool.wait_ge(rB_ready, 3)
            pool.wait_ge(down_v, MT)
            for jj in range(OUT_V, MT // 2):
                y2, x2 = yT[:, 2 * jj:2 * jj + 2], xT[:, 2 * jj:2 * jj + 2]
                line.step(G.tensor_tensor(y2, y2, rB[:].unsqueeze(1).to_broadcast([P, 2, TOK]), ALU.mult))
                G.tensor_tensor(y2, y2, x2, ALU.add).then_inc(out_ready[jj], 1)
            pool.wait_ge(other_stored, 32)
            pool.wait_ge(kv_stored[0], 32)
            pool.wait_ge(kv_stored[1], 32)
            pool.wait_ge(v_stored, 16 * 5)

        @block.tensor
        def _(pe):
            def mm3(out, w, x, xl, start, stop):
                slot, c = w
                a, b = wh[:, slot, c:c + P], wl[:, slot, c:c + P]
                nc.tensor.matmul(out, a, x, start=start, stop=False)
                nc.tensor.matmul(out, a, xl, start=False, stop=False)
                return nc.tensor.matmul(out, b, x, start=False, stop=stop)

            def gemm(c, bank, xh, xl, kt0, first, last, split=None):
                n, slot, _ = c
                pe.wait_ge(lo_ready, n + 1)
                for k in range(4):
                    if split is not None:
                        pe.wait_ge(split, kt0 + k + 1)
                    for m in range(2):
                        ins = mm3(ps[:, bank + m, 0:TOK], (slot, 256 * k + P * m), xh[:, kt0 + k], xl[:, kt0 + k],
                                  first and k == 0, last and k == 3)
                ins.then_inc(weights_used, 1)
                return ins

            def take_misc(kind, *a):
                n = misc(kind, *a)
                if n:
                    pe.wait_ge(misc_free, n)

            def stage(kind, *a):
                if kind == "ss":
                    pe.wait_ge(const_ready, 2)
                    for j in range(MT):
                        if j % 4 == 0:
                            pe.wait_ge(xsq_ready, j // 4 + 1)
                        ins = nc.tensor.matmul(ps[:, B_M, 0:TOK], ones[:], xsq[:, j], start=j == 0, stop=j == MT - 1)
                    ins.then_inc(misc_ready, 1)
                elif kind == "qk":
                    t, = a
                    pe.wait_ge(tab_landed, 32)
                    pe.wait_ge(evac_done, GI[("kB", t)] + 1)
                    take_misc(kind, *a)
                    for c, src in enumerate((qs, ks)):
                        for m in range(2):
                            ins = nc.tensor.transpose(ps[0:NDEC, B_M, 256 * c + P * m:256 * c + P * m + P],
                                                      src[:, t % 2, m, SEQ:TOK], ident[:])
                    ins.then_inc(misc_ready, 1)
                elif kind == "vtr":
                    T, = a
                    pe.wait_ge(evac_done, GI[("vB", T) if T < 4 else ("kvA", 0)] + 1)
                    take_misc(kind, *a)
                    w = 2 if T < 4 else 1
                    for b in range(2):
                        for m in range(w):
                            ins = nc.tensor.transpose(ps[:, B_M, (b * w + m) * P:(b * w + m + 1) * P],
                                                      vT[:, m, P * b:P * b + P], ident[:])
                    ins.then_inc(misc_ready, 1)
                elif kind == "vdec":
                    take_misc(kind, *a)
                    nc.tensor.transpose(ps[0:NDEC, B_M, 0:P], vT[:, 0, SEQ:TOK], ident[:]).then_inc(misc_ready, 1)
                elif kind == "S":
                    T, h = a
                    n = number(kind, *a)
                    pe.wait_ge(evac_done, (GI[("kB", T)] if T < 4 else q_group(T)) + 1)
                    if n > 1:
                        pe.wait_ge(masked_ready, n - 1)
                    half, m = heads_of(T, h)
                    q = qs[half, T % 2, m]
                    k = ks[half, T % 2, m] if T < 4 else kdup[half, (T - 4) // 2]
                    nc.tensor.matmul(ps[:, B_S, 0:P], q[:, 0:P], k[:, 0:P], start=True, stop=True)
                    nc.tensor.matmul(ps[:, B_S, P:384], q[:, P:SEQ], k[:, 0:SEQ], start=True,
                                     stop=True).then_inc(scores_ready, 1)
                elif kind == "T":
                    n = number(kind, *a)
                    pe.wait_ge(exp_ready, n)
                    if n > 1:
                        pe.wait_ge(pt_copied, n - 1)
                    for c in range(3):
                        ins = nc.tensor.transpose(ps[:, B_T, P * c:P * c + P], Sm[:, n % 2, P * c:P * c + P], ident[:])
                    ins.then_inc(pt_ready, 1)
                elif kind == "V":
                    T, h = a
                    n = number(kind, *a)
                    pe.wait_ge(pt_copied, n)
                    if h == 0:
                        pe.wait_ge(misc_free, misc("vtr", min(T, 4)) + 1)
                        if T:
                            pe.wait_ge(o_taken, T)
                    if T < 4:
                        v = [vn[:, T % 2, b, HD * h:HD * h + HD] for b in range(2)]
                    else:
                        c = HD * ((T - 4) // 2)
                        v = [vnA[:, b, c:c + HD] for b in range(2)]
                    o = [ps[:, B_O, 256 * b + HD * h:256 * b + HD * h + HD] for b in range(2)]
                    pt = PT[:, n % 2]
                    nc.tensor.matmul(o[0], pt[:, 0:P], v[0], start=True, stop=True)
                    nc.tensor.matmul(o[1], pt[:, P:2 * P], v[0], start=True, stop=False)
                    nc.tensor.matmul(o[1], pt[:, 2 * P:384], v[1], start=False, stop=True).then_inc(pv_ready, 1)
                elif kind == "aS":
                    pe.wait_ge(evac_done, GI[("qA", 3)] + 1)
                    pe.wait_ge(aq_ready, 1)
                    take_misc(kind, *a)
                    for c, (k0, k1) in enumerate(KSPLIT_A):
                        for s in range(NDEC):
                            ins = nc.tensor.matmul(ps[0:k1 - k0, B_M, P * c + H_A * s:P * c + H_A * s + H_A],
                                                   KtA[:, s, k0:k1], qA[:, s], start=True, stop=True)
                    ins.then_inc(misc_ready, 1)
                elif kind == "aT":
                    take_misc(kind, *a)
                    for c, (k0, k1) in enumerate(KSPLIT_A):
                        ins = nc.tensor.transpose(ps[:, B_M, k0:k1], aSc[0:k1 - k0, P * c:P * c + P],
                                                  ident[0:k1 - k0, 0:k1 - k0])
                    ins.then_inc(misc_ready, 1)
                elif kind == "aR":
                    pe.wait_ge(a_p, 1)
                    take_misc(kind, *a)
                    for c, (k0, k1) in enumerate(KSPLIT_A):
                        ins = nc.tensor.transpose(ps[0:k1 - k0, B_M, P * c:P * c + P], aP[:, k0:k1], ident[:])
                    ins.then_inc(misc_ready, 1)
                elif kind == "aV":
                    pe.wait_ge(VtA_full, 16)
                    take_misc(kind, *a)
                    for s in range(NDEC):
                        for c, (k0, k1) in enumerate(KSPLIT_A):
                            ins = nc.tensor.matmul(ps[:, B_M, H_A * s:H_A * s + H_A], VtA[0:k1 - k0, c, s],
                                                   aPT[0:k1 - k0, P * c + H_A * s:P * c + H_A * s + H_A],
                                                   start=c == 0, stop=c == 1)
                    ins.then_inc(misc_ready, 1)
                elif kind == "bT":
                    pe.wait_ge(bS_ready, a[0] + 1)
                    take_misc(kind, *a)
                    for c, (k0, k1) in enumerate(KSPLIT_B):
                        ins = nc.tensor.transpose(ps[0:16, B_M, k0:k1], bSc[0:k1 - k0, 16 * c:16 * c + 16],
                                                  ident[0:k1 - k0, 0:k1 - k0])
                    ins.then_inc(misc_ready, 1)
                elif kind == "W":
                    X, j = a
                    pe.wait_ge(onat_scaled, X + 1)
                    take_misc(kind, *a)
                    for b in range(2):
                        ins = nc.tensor.transpose(ps[:, B_M, P * b:P * b + P], onat[:, b, P * j:P * j + P], ident[:])
                    ins.then_inc(misc_ready, 1)
                elif kind == "ND":
                    X, = a
                    pe.wait_ge(od_sq, X + 1)
                    take_misc(kind, *a)
                    nc.tensor.matmul(ps[:, B_M, 0:OT * NDEC], ones[:], od[:, 1].rearrange("p j s -> p (j s)"),
                                     start=True, stop=True).then_inc(misc_ready, 1)

            def sum_squares(c, last):
                pe.wait_ge(ysq_used, SUMS * (c + 1))
                for k in range(2):
                    nc.tensor.matmul(ps[:, B_M, 0:TOK], ones[:], sqa[:, k], start=k == 0, stop=False)
                pe.wait_ge(ysq_ready, 8 * (c + 1))
                for k in range(2):
                    ins = nc.tensor.matmul(ps[:, B_M, 0:TOK], ones[:], last[:, k], start=False, stop=k == 1)
                ins.then_inc(sum_ready, 1)

            for n in range(N_ATT):
                if n < N_IN:
                    gi, c = n // 4, n % 4
                    if c == 0 and gi >= 2:
                        pe.wait_ge(evac_done, gi - 1)
                    gemm(chunk(0, 0, 4, n), 2 * (gi % 2), hh, hl, 4 * c, c == 0, c == 3,
                         xl_ready if gi == 0 else None)
                else:
                    g, c = (n - N_IN) // 2, (n - N_IN) % 2
                    gi = G_IN + g
                    if c == 0:
                        pe.wait_ge(evac_done, gi - 1)
                    if n == N_IN:
                        pe.wait_ge(misc_free, misc("ND", 0) + 1)
                    gemm(chunk(0, 0, 4, n), 2 * (gi % 2), oBh, oBl, 4 * c, c == 0, c == 1)
                for s in PLAN[n]:
                    stage(*s)
            for s in PLAN[N_ATT]:
                stage(*s)

            pe.wait_ge(misc_free, len(MISC))
            with pe.Fori(0, G_OUT // 2) as i:
                for g in range(2):
                    pe.wait_ge(evac_done, i * 2 + (G_IN + G_OUT + g - 1))
                    for c in range(2):
                        gemm(chunk(B_OUTB, i, 4, 2 * g + c), 2 * ((G_IN + G_OUT + g) % 2), hh, hh[:, OT:2 * OT],
                             4 * c, c == 0, c == 1)
            sum_squares(0, sq)

            def ffn(i, first):
                if not first:
                    pe.wait_ge(u_ready, i)
                for c in range(4):
                    gemm(chunk(B_GU, i, 8, c), 0, hh, hl, 4 * c, c == 0, c == 3, h2l_ready if first else None)
                if not first:
                    pe.wait_ge(up_taken, i)
                for c in range(4):
                    gemm(chunk(B_GU, i, 8, 4 + c), 2, hh, hl, 4 * c, c == 0, c == 3)
                    if first and c == 1:
                        sum_squares(1, sq2)

            ffn(0, True)
            with pe.Fori(0, G_FF - 1) as i:
                ffn(i + 1, False)

            def down(c, kt, first, last, half):
                n, slot, _ = c
                pe.wait_ge(lo_ready, n + 1)
                for m in range(8):
                    if first and half == 0 and m == 4:
                        pe.wait_ge(u_ready, G_FF)
                    if first and half == 0 and m == 6:
                        pe.wait_ge(up_taken, G_FF)
                    if first and half == 1:
                        pe.wait_ge(down_v, m + 1)
                    ins = mm3(ps[:, (m + 4) % 8, 0:TOK], (slot, P * m), gh[:, kt], gl[:, kt], first, last)
                    if last and m < 7:
                        ins.then_inc(down_done, 1)
                ins.then_inc(weights_used, 1)

            for half in range(2):
                base = B_DOWN + FT * half
                for j in range(4):
                    if half == 0 and j % 2 == 0:
                        pe.wait_ge(gl_ready, j // 2 + 1)
                    down(chunk(base, 0, 4, j), j, j == 0, False, half)
                with pe.Fori(0, FT // 4 - 2) as i:
                    if half == 0:
                        pe.wait_ge(gl_ready, i * 2 + 4)
                    for j in range(4):
                        down(chunk(base + 4, i, 4, j), i * 4 + (4 + j), False, False, half)
                if half == 0:
                    pe.wait_ge(gl_ready, G_FF)
                for j in range(4):
                    down(chunk(base, FT // 4 - 1, 4, j), FT - 4 + j, False, j == 3, half)
            pe.wait_ge(ysq_used, 2 * SUMS + 1 + 5)
            pe.wait_ge(down_v, MT // 2 + 1)
            for k in range(2):
                nc.tensor.matmul(ps[:, 4, 0:TOK], ones[:], sqa[:, k], start=k == 0, stop=False)
            for j in range(MT - 6, MT):
                pe.wait_ge(ysq2_ready, j + 1)
                ins = nc.tensor.matmul(ps[:, 4, 0:TOK], ones[:], ysq[:, j], start=False, stop=j == MT - 1)
            ins.then_inc(sum_ready, 1)


def shape_tables():
    tab = np.zeros((P, N_TAB), np.float32)
    q = np.arange(P)[:, None]

    def count(dist):
        return sum(((dist >= 0) & (dist <= w) & (dist % s == 0)).astype(int) for w, s in DILATIONS)

    def cost(c):
        return np.where(c > 0, -np.log(np.maximum(c, 1)), NEG).astype(np.float32)

    dist = np.concatenate([q - np.arange(P)[None], P + q - np.arange(2 * P)[None]], axis=1)
    tab[:, T_MA:T_MA + 384] = cost(((dist >= 0) & (dist <= WINDOW_A)).astype(int))
    tab[:, T_MB:T_MB + 384] = cost(count(dist))
    tab[:, T_MD:T_MD + KB] = cost(count(np.concatenate([rows_b_dist(), [0]])))[None]
    half = ROT // 2
    inv = np.float32(THETA) ** (-np.arange(half, dtype=np.float32) * np.float32(2.0 / ROT))
    pos = np.concatenate([np.arange(SEQ), np.full(NDEC, PAST)]).astype(np.float32)
    ang = (pos[:, None] * inv[None]).astype(np.float32).astype(np.float64)
    cos, sin = np.cos(ang).T.astype(np.float32), np.sin(ang).T.astype(np.float32)
    for o in (0, HD):
        tab[o:o + HD, T_COS:T_COS + TOK] = 1.0
        tab[o:o + half, T_COS:T_COS + TOK] = cos
        tab[o + half:o + ROT, T_COS:T_COS + TOK] = cos
        tab[o:o + half, T_SIN:T_SIN + TOK] = -sin
        tab[o + half:o + ROT, T_SIN:T_SIN + TOK] = sin
    return tab


def rows_b_dist():
    dist = set()
    for w, s in DILATIONS:
        dist |= set(range(s, w + 1, s))
    return np.array(sorted(dist, reverse=True))


def kernel(**inputs):
    import concourse.bacc as bacc
    from concourse.bass_utils import run_bass_kernel_spmd

    v = {k: np.asarray(a) for k, a in inputs.items()}
    asc = np.ascontiguousarray

    def cols(a, n):
        return np.reshape(a, (n, P)).T

    x = np.concatenate([v["x_prompt"][0], v["x_sample"][:, 0]], axis=0)
    arrays = {
        "x": asc(x.T.reshape(MT, P, TOK).transpose(1, 0, 2)),
        "ident": np.eye(P, dtype=np.float32),
        "tab": shape_tables(),
    }
    st = v["state_conv"][0].transpose(2, 0, 1).reshape(FT, P, NDEC, 2).transpose(1, 0, 2, 3)
    sinks = v["attn_sinks"][0].reshape(H_A)
    arrays["par"] = asc(np.concatenate([
        cols(v["g_pre_mix"][0], MT), cols(v["g_post_mix"][0], MT), cols(v["g_pre_ffn"][0], MT),
        cols(v["g_post_ffn"][0], MT), cols(v["g_out_b"][0], OT), cols(v["g_out_a"][0], OT),
        *[cols(v["conv_w"][0, j], FT) for j in range(3)], cols(v["conv_b"][0], FT),
        st.reshape(P, FT * 2 * NDEC), np.broadcast_to(sinks, (P, H_A)), np.tile(sinks, NDEC)[:, None],
    ], axis=1))
    w = v["w_in"][0].reshape(4, 4, P, G_IN, 256)
    arrays["w_in"] = asc(w.transpose(3, 0, 2, 1, 4)).reshape(G_IN, 4, P, CH)
    w = v["w_out"][0].reshape(2, 2, 4, P, G_OUT, 256)
    arrays["w_out"] = asc(w[::-1].transpose(0, 4, 1, 3, 2, 5)).reshape(4 * G_OUT, P, CH)
    for n in ("w_gate", "w_up"):
        w = v[n][0].reshape(4, 4, P, G_FF, 256)
        arrays[n] = asc(w.transpose(3, 0, 2, 1, 4)).reshape(4 * G_FF, P, CH)
    w = v["w_down"][0].reshape(FT, P, 2, CH)
    arrays["w_down"] = asc(w.transpose(2, 0, 1, 3)).reshape(2 * FT, P, CH)
    k = v["cache_a_k"][0].reshape(NDEC, WINDOW_A, P).transpose(2, 0, 1)
    arrays["ka"] = asc(np.concatenate([k[:, :, 0:64], np.zeros((P, NDEC, 1), np.float32), k[:, :, 64:]], axis=2))
    arrays["va"] = asc(v["cache_a_v"][0].reshape(NDEC, 2, 64, P).transpose(2, 1, 0, 3))
    rows = PAST - rows_b_dist()
    k = v["cache_b_k"][0][:, rows].reshape(NDEC, KEYS_B, OT, P)
    k = np.concatenate([k, np.zeros((NDEC, 384 - KEYS_B, OT, P), np.float32)], axis=1)
    arrays["kb"] = asc(k.reshape(NDEC, 3, P, OT, P).transpose(3, 2, 1, 0, 4))
    arrays["vb"] = asc(v["cache_b_v"][0][:, rows].reshape(NDEC, KEYS_B, OT, P).transpose(2, 3, 0, 1))
    outs = {
        "out_y": (P, MT, TOK), "out_ka": (P, TOK), "out_va": (P, TOK),
        "out_kb": (4, P, 2, TOK), "out_vb": (4, P, 2, TOK), "out_conv": (P, FT, 2 + 2 * NDEC),
    }
    nc = bacc.Bacc("TRN2", target_bir_lowering=False, num_devices=1)
    d = {n: nc.dram_tensor("in_" + n, a.shape, F32, kind="ExternalInput").ap() for n, a in arrays.items()}
    d.update({n: nc.dram_tensor(n, s, F32, kind="ExternalOutput").ap() for n, s in outs.items()})
    build(nc, d, nc.dram_tensor("q_dram", (4, NDEC, 256), F32, kind="Internal").ap(),
          nc.dram_tensor("p_dram", (OT, 16, KB), F32, kind="Internal").ap())
    r = run_bass_kernel_spmd(nc, [{"in_" + n: a for n, a in arrays.items()}], core_ids=[0]).results[0]

    y = r["out_y"].transpose(2, 1, 0).reshape(TOK, D_MODEL)
    ka, va = r["out_ka"].T.reshape(TOK, KV_A, HD), r["out_va"].T.reshape(TOK, KV_A, HD)
    kb, vb = (r[n].transpose(3, 0, 2, 1).reshape(TOK, H_B, HD) for n in ("out_kb", "out_vb"))
    cv = r["out_conv"].transpose(1, 0, 2).reshape(D_FF, 2 + 2 * NDEC)
    last = SEQ - WINDOW_A
    return (
        asc(y[None, :SEQ]), asc(y[SEQ:, None]),
        asc(ka[None, None, last:SEQ]), asc(va[None, None, last:SEQ]),
        asc(kb[None, None, :SEQ]), asc(vb[None, None, :SEQ]),
        asc(cv[:, 0:2].T[None, None]),
        asc(ka[None, SEQ:, None]), asc(va[None, SEQ:, None]),
        asc(kb[None, SEQ:, None]), asc(vb[None, SEQ:, None]),
        asc(cv[:, 2:].reshape(D_FF, NDEC, 2).transpose(1, 2, 0)[None]),
    )
```
